# Optimizing a Trainium2 kernel written in Bass

```python
import jax, jax.numpy as jnp
from jax import lax
import numpy as np

D_MODEL = 1024
BATCH = 1
SEQ = 512
DEPTH = 2

GRID_W = 64
CTX_LEN = 256
HEAD_DIM = 64
MIX_W = D_MODEL
POOL_W = MIX_W // 4
POOL_WINDOWS = (2, 4, 8, 16)
POOL_GW = POOL_W // len(POOL_WINDOWS)
ATT_W = MIX_W // 2
ATT_HEADS = ATT_W // HEAD_DIM
ATT_KV_HEADS = max(1, ATT_HEADS // 4)
ATT_GROUP = ATT_HEADS // ATT_KV_HEADS
ATT_KV_W = ATT_KV_HEADS * HEAD_DIM
WINDOW = 128
ATT_BLOCK = 128
HG_VW = MIX_W - POOL_W - ATT_W
HG_HEADS = HG_VW // HEAD_DIM
HG_DK = HEAD_DIM
HG_DV = HEAD_DIM
HG_KW = HG_HEADS * HG_DK
HG_CHUNK = 64
IN_SIZES = (POOL_W, ATT_W, ATT_KV_W, ATT_KV_W, HG_KW, HG_KW, HG_KW, HG_VW, HG_VW)
IN_W = sum(IN_SIZES)
D_FF = 4 * D_MODEL
ROPE_BASE = 10000.0
EPS = 1e-6
NEG_BIG = -1e30

kernel_name = "hybrid_pool_swa_hgrn2_prefix_dit"

def rmsnorm(x, w):
    xf = x.astype(jnp.float32)
    y = xf * lax.rsqrt(jnp.mean(xf * xf, axis=-1, keepdims=True) + EPS)
    return (y * w.astype(jnp.float32)).astype(x.dtype)

def axial_rope_tables(n):
    rows_n = n // GRID_W
    row = jnp.repeat(jnp.arange(rows_n), GRID_W).astype(jnp.float32)
    col = jnp.tile(jnp.arange(GRID_W), rows_n).astype(jnp.float32)
    axis_dims = HEAD_DIM // 2
    inv = ROPE_BASE ** (-jnp.arange(0, axis_dims, 2, dtype=jnp.float32) / axis_dims)
    ar = row[:, None] * inv
    ac = col[:, None] * inv
    return (jnp.cos(ar), jnp.sin(ar), jnp.cos(ac), jnp.sin(ac))

def _rot_half(x, cos, sin):
    x1, x2 = jnp.split(x, 2, axis=-1)
    c = cos[:, None, :]
    s = sin[:, None, :]
    return jnp.concatenate([x1 * c - x2 * s, x2 * c + x1 * s], axis=-1)

def apply_axial_rope(x, tabs):
    cr, sr, cc, sc = tabs
    xr, xc = jnp.split(x, 2, axis=-1)
    return jnp.concatenate([_rot_half(xr, cr, sr), _rot_half(xc, cc, sc)], axis=-1).astype(x.dtype)

def split_in(z):
    idx = np.cumsum(IN_SIZES)[:-1].tolist()
    return jnp.split(z, idx, axis=-1)

def pool_mixer(u, pool_w, pool_scale):
    B, n, _ = u.shape
    uf = u.astype(jnp.float32)
    csum = jnp.concatenate([jnp.zeros_like(uf[:, :1]), jnp.cumsum(uf, axis=1)], axis=1)
    pos = jnp.arange(n)
    outs = []
    for g, w in enumerate(POOL_WINDOWS):
        lo = jnp.clip(pos - w // 2, 0, n)
        hi = jnp.clip(pos + w // 2, 0, n)
        cg = csum[..., g * POOL_GW:(g + 1) * POOL_GW]
        cnt = (hi - lo).astype(jnp.float32)[None, :, None]
        outs.append((cg[:, hi] - cg[:, lo]) / cnt)
    d = jnp.concatenate(outs, axis=-1) - uf
    d = d.reshape(B, n, len(POOL_WINDOWS), POOL_GW)
    y = jnp.einsum('bngc,gcd->bngd', d, pool_w.astype(jnp.float32)).reshape(B, n, POOL_W)
    return (y * pool_scale.astype(jnp.float32)).astype(u.dtype)

def softmax_with_sink(s, sink):
    sk = jnp.broadcast_to(sink.astype(jnp.float32)[:, :, None, None], s.shape[:-1] + (1,))
    p = jax.nn.softmax(jnp.concatenate([s, sk], axis=-1), axis=-1)
    return p[..., :-1]

def window_attention(q, k, v, kc, vc, sink):
    B, S = q.shape[:2]
    L = kc.shape[1]
    nb = S // ATT_BLOCK
    qb = q.reshape(B, nb, ATT_BLOCK, ATT_KV_HEADS, ATT_GROUP, HEAD_DIM)
    pad = ((0, 0), (ATT_BLOCK, ATT_BLOCK), (0, 0), (0, 0))
    kp = jnp.pad(k, pad)
    vp = jnp.pad(v, pad)

    def bands(a):
        return jnp.concatenate([a[:, i * ATT_BLOCK:i * ATT_BLOCK + S].reshape(B, nb, ATT_BLOCK, ATT_KV_HEADS, HEAD_DIM)
                                for i in range(3)], axis=2)

    kb, vb = bands(kp), bands(vp)
    scale = HEAD_DIM ** -0.5
    s_loc = jnp.einsum('bnqkgd,bnskd->bnkgqs', qb, kb).astype(jnp.float32) * scale
    s_ctx = jnp.einsum('bnqkgd,bskd->bnkgqs', qb, kc).astype(jnp.float32) * scale
    qpos = jnp.arange(S).reshape(nb, ATT_BLOCK)
    kpos = jnp.arange(nb)[:, None] * ATT_BLOCK - ATT_BLOCK + jnp.arange(3 * ATT_BLOCK)[None, :]
    valid = ((kpos[:, None, :] >= 0) & (kpos[:, None, :] < S)
             & (jnp.abs(qpos[:, :, None] - kpos[:, None, :]) <= WINDOW))
    s_loc = jnp.where(valid[None, :, None, None], s_loc, NEG_BIG)
    p = softmax_with_sink(jnp.concatenate([s_loc, s_ctx], axis=-1), sink.reshape(ATT_KV_HEADS, ATT_GROUP))
    nk = 3 * ATT_BLOCK
    p_loc = p[..., :nk].astype(v.dtype)
    p_ctx = p[..., nk:nk + L].astype(v.dtype)
    o = (jnp.einsum('bnkgqs,bnskd->bnqkgd', p_loc, vb)
         + jnp.einsum('bnkgqs,bskd->bnqkgd', p_ctx, vc))
    return o.reshape(B, S, ATT_W)

def context_attention(qc, kc, vc, sink):
    B, L = qc.shape[:2]
    qg = qc.reshape(B, L, ATT_KV_HEADS, ATT_GROUP, HEAD_DIM)
    s = jnp.einsum('blkgd,bskd->bkgls', qg, kc).astype(jnp.float32) * (HEAD_DIM ** -0.5)
    p = softmax_with_sink(s, sink.reshape(ATT_KV_HEADS, ATT_GROUP)).astype(vc.dtype)
    return jnp.einsum('bkgls,bskd->blkgd', p, vc).reshape(B, L, ATT_W)

def gla_chunk_scan(q, k, v, logf, s0):
    B, n, H, _ = q.shape
    nc = n // HG_CHUNK

    def to_chunks(a):
        return jnp.moveaxis(a.reshape(B, nc, HG_CHUNK, H, a.shape[-1]), 1, 0)

    tri = jnp.tril(jnp.ones((HG_CHUNK, HG_CHUNK), dtype=bool))[None, :, :, None, None]

    def step(S, inp):
        qc, kc, vc, gc = inp
        b = jnp.cumsum(gc, axis=1)
        diff = jnp.where(tri, b[:, :, None] - b[:, None, :], NEG_BIG)
        a = jnp.sum(qc[:, :, None] * kc[:, None] * jnp.exp(diff), axis=-1)
        o = jnp.einsum('btsh,bshv->bthv', a, vc) + jnp.einsum('bthk,bhkv->bthv', qc * jnp.exp(b), S)
        b_end = b[:, -1]
        S_new = (jnp.exp(b_end)[..., None] * S
                 + jnp.einsum('bshk,bshv->bhkv', kc * jnp.exp(b_end[:, None] - b), vc))
        return S_new, o

    s_fin, o = lax.scan(step, s0, (to_chunks(q), to_chunks(k), to_chunks(v), to_chunks(logf)))
    return jnp.moveaxis(o, 0, 1).reshape(B, n, H, v.shape[-1]), s_fin

def _heads(a):
    B, n = a.shape[:2]
    return a.astype(jnp.float32).reshape(B, n, HG_HEADS, -1)

def hgrn2_gates(f_pre, lb):
    lb = lb.astype(jnp.float32)
    f = lb + (1.0 - lb) * jax.nn.sigmoid(f_pre.astype(jnp.float32))
    return _heads(1.0 - f), _heads(jnp.log(f))

def hgrn2_mixer(q, ff, fb, i, g, cq, cff, cfb, ci, cg, lb_f, lb_b, norm_w, need_ctx):
    B = q.shape[0]
    s0 = jnp.zeros((B, HG_HEADS, HG_DK, HG_DV), jnp.float32)
    flip = lambda a: jnp.flip(a, axis=1)
    qh, vh = _heads(jax.nn.silu(q)), _heads(i)
    cqh, cvh = _heads(jax.nn.silu(cq)), _heads(ci)
    kf, gf = hgrn2_gates(ff, lb_f)
    ckf, cgf = hgrn2_gates(cff, lb_f)
    oc_f, sc_f = gla_chunk_scan(cqh, ckf, cvh, cgf, s0)
    o_f, _ = gla_chunk_scan(qh, kf, vh, gf, sc_f)
    kb, gb = hgrn2_gates(fb, lb_b)
    ckb, cgb = hgrn2_gates(cfb, lb_b)
    oc_b, sc_b = gla_chunk_scan(flip(cqh), flip(ckb), flip(cvh), flip(cgb), s0)
    o_b, _ = gla_chunk_scan(flip(qh), flip(kb), flip(vh), flip(gb), sc_b)

    def readout(o, gate):
        Bn, n = o.shape[:2]
        return (rmsnorm(o, norm_w).reshape(Bn, n, HG_VW) * jax.nn.silu(gate.astype(jnp.float32))).astype(gate.dtype)

    y = readout(o_f + flip(o_b), g)
    yc = readout(oc_f + flip(oc_b), cg) if need_ctx else None
    return y, yc

def token_mixer(h, hc, w_in, pool_w, pool_scale, sink, lb_f, lb_b, hg_norm_w, w_out, rope, need_ctx):
    B, S, _ = h.shape
    L = hc.shape[1]
    pa, qa, ka, va, qh, ff, fb, ih, gh = split_in(h @ w_in)
    cpa, cqa, cka, cva, cqh, cff, cfb, cih, cgh = split_in(hc @ w_in)
    ya = pool_mixer(pa, pool_w, pool_scale)
    q = apply_axial_rope(qa.reshape(B, S, ATT_HEADS, HEAD_DIM), rope)
    k = apply_axial_rope(ka.reshape(B, S, ATT_KV_HEADS, HEAD_DIM), rope)
    v = va.reshape(B, S, ATT_KV_HEADS, HEAD_DIM)
    kc = cka.reshape(B, L, ATT_KV_HEADS, HEAD_DIM)
    vc = cva.reshape(B, L, ATT_KV_HEADS, HEAD_DIM)
    yb = window_attention(q, k, v, kc, vc, sink)
    yc, ycc = hgrn2_mixer(qh, ff, fb, ih, gh, cqh, cff, cfb, cih, cgh, lb_f, lb_b, hg_norm_w, need_ctx)
    y = jnp.concatenate([ya, yb, yc], axis=-1) @ w_out
    if not need_ctx:
        return y, None
    yca = pool_mixer(cpa, pool_w, pool_scale)
    ycb = context_attention(cqa.reshape(B, L, ATT_HEADS, HEAD_DIM), kc, vc, sink)
    y_ctx = jnp.concatenate([yca, ycb, ycc], axis=-1) @ w_out
    return y, y_ctx

def sqrelu_mlp(h, w1, w2):
    return jnp.square(jax.nn.relu(h @ w1)) @ w2

def setup_inputs(seed: int = 0) -> dict:
    key = jax.random.key(seed)
    ks = jax.random.split(key, 20)
    nrm = lambda k, shape, s: jax.random.normal(k, shape, jnp.float32) * s
    return {
        'x': nrm(ks[0], (BATCH, SEQ, D_MODEL), 1.0),
        'c': nrm(ks[1], (BATCH, D_MODEL), 1.0),
        'ctx': nrm(ks[2], (BATCH, CTX_LEN, D_MODEL), 1.0),
        'c_ctx': nrm(ks[3], (D_MODEL,), 1.0),
        'w_ada': nrm(ks[4], (DEPTH, D_MODEL, 6 * D_MODEL), D_MODEL ** -0.5),
        'b_ada': nrm(ks[5], (DEPTH, 6 * D_MODEL), 0.02),
        'norm1_w': 1.0 + nrm(ks[6], (DEPTH, D_MODEL), 0.1),
        'w_in': nrm(ks[7], (DEPTH, D_MODEL, IN_W), D_MODEL ** -0.5),
        'pool_w': nrm(ks[8], (DEPTH, len(POOL_WINDOWS), POOL_GW, POOL_GW), POOL_GW ** -0.5),
        'pool_scale': 1.0 + nrm(ks[9], (DEPTH, POOL_W), 0.1),
        'attn_sink': nrm(ks[10], (DEPTH, ATT_HEADS), 0.5),
        'hg_lower': nrm(ks[11], (DEPTH, 2, HG_KW), 0.5),
        'hg_norm_w': 1.0 + nrm(ks[12], (DEPTH, HG_DV), 0.1),
        'w_out': nrm(ks[13], (DEPTH, MIX_W, D_MODEL), MIX_W ** -0.5),
        'norm2_w': 1.0 + nrm(ks[14], (DEPTH, D_MODEL), 0.1),
        'w_mlp1': nrm(ks[15], (DEPTH, D_MODEL, D_FF), D_MODEL ** -0.5),
        'w_mlp2': nrm(ks[16], (DEPTH, D_FF, D_MODEL), D_FF ** -0.5),
        'final_norm_w': 1.0 + nrm(ks[17], (D_MODEL,), 0.1),
    }

def reference(x, c, ctx, c_ctx, w_ada, b_ada, norm1_w, w_in, pool_w, pool_scale, attn_sink,
              hg_lower, hg_norm_w, w_out, norm2_w, w_mlp1, w_mlp2, final_norm_w):
    rope = axial_rope_tables(x.shape[1])
    lbs = jax.nn.softmax(hg_lower.astype(jnp.float32), axis=0)
    lbs = jnp.cumsum(lbs, axis=0) - lbs[0]
    sc_lat = jax.nn.silu(c)
    sc_ctx = jax.nn.silu(c_ctx)
    xc = ctx
    for l in range(DEPTH):
        need_ctx = l < DEPTH - 1
        m = (sc_lat @ w_ada[l] + b_ada[l])[:, None, :]
        mc = sc_ctx @ w_ada[l] + b_ada[l]
        sh1, s1, g1, sh2, s2, g2 = jnp.split(m, 6, axis=-1)
        csh1, cs1, cg1, csh2, cs2, cg2 = jnp.split(mc, 6, axis=-1)
        h = rmsnorm(x, norm1_w[l]) * (1.0 + s1) + sh1
        hc = rmsnorm(xc, norm1_w[l]) * (1.0 + cs1) + csh1
        y, y_ctx = token_mixer(h, hc, w_in[l], pool_w[l], pool_scale[l], attn_sink[l],
                               lbs[l, 0], lbs[l, 1], hg_norm_w[l], w_out[l], rope, need_ctx)
        x = x + g1 * y
        h = rmsnorm(x, norm2_w[l]) * (1.0 + s2) + sh2
        x = x + g2 * sqrelu_mlp(h, w_mlp1[l], w_mlp2[l])
        if need_ctx:
            xc = xc + cg1 * y_ctx
            hc = rmsnorm(xc, norm2_w[l]) * (1.0 + cs2) + csh2
            xc = xc + cg2 * sqrelu_mlp(hc, w_mlp1[l], w_mlp2[l])
    return rmsnorm(x, final_norm_w)


_drawn_inputs = setup_inputs


def setup_inputs(seed=0):
    import zlib

    import numpy as np

    out = dict(_drawn_inputs(seed))
    spreads = {}
    factors = {'attn_sink': 8.0, 'hg_lower': 8.0}
    for name, (base, spread) in spreads.items():
        noise = np.random.default_rng([zlib.crc32(name.encode()), seed]).standard_normal(out[name].shape)
        drawn = base * np.exp(spread * noise) if base else spread * noise
        out[name] = __import__('jax').numpy.asarray(drawn.astype(out[name].dtype))
    for name, factor in factors.items():
        out[name] = (out[name] * factor).astype(out[name].dtype)
    return out
```

```python
from contextlib import ExitStack

import numpy as np
import concourse.bass as bass
from concourse import mybir

F32, F16, BF16, U8 = mybir.dt.float32, mybir.dt.float16, mybir.dt.bfloat16, mybir.dt.uint8
ALU = mybir.AluOpType
ACT = mybir.ActivationFunctionType
AX_X = mybir.AxisListType.X

P = 128
D = 1024
KC = D // P
LAT, CTX = 512, 256
TOK = LAT + CTX
NB = TOK // P
LB = LAT // P
DEPTH = 2
HD = 64
QH, KVH = 8, 2
FF = 4 * D
FU = FF // P
EPS = 1e-6
GRID_W = 64
POOL_WINDOWS = (2, 4, 8, 16)

W_SCALE = 256.0
A_SCALE = 64.0
H_SCALE = 1.0
UNSCALE = 1.0 / (W_SCALE * A_SCALE)
UNSCALE2 = 1.0 / (W_SCALE * H_SCALE)

RING = 4
AHEAD = 2
UNIT = KC * P
N_IN, N_OUT, N_UP, N_DOWN = 18, KC, FU, KC * (FF // D)
ADA_BLOCKS = 6 * D // 512
IN_ORDER = [("pool", 0), ("pool", 1), ("ff", 0), ("ff", 1), ("fb", 0), ("fb", 1), ("qh", 0), ("qh", 1),
            ("ih", 0), ("ih", 1), ("k", 0), ("va", 0), ("q", 0), ("q", 1), ("q", 2), ("q", 3), ("gh", 0), ("gh", 1)]
TOKEN_MAJOR = ("ih", "va")
CTX_NEEDED_LAST = ("ff", "fb", "ih", "k", "va")


def plan_stream():
    out, w, a = [], 0, 0

    def weight():
        nonlocal w
        if w < DEPTH * (N_IN + N_OUT + N_UP + N_DOWN):
            out.append(("w", w))
            w += 1

    def ada(n):
        nonlocal a
        out.extend(("a", a + i) for i in range(n))
        a += n

    ada(16)
    for _ in range(AHEAD):
        weight()
    for l in range(DEPTH):
        for i in range(N_IN):
            weight()
            if l == 0 and i < 16:
                ada(2)
        for _ in range(N_OUT):
            weight()
        for _ in range(N_UP):
            weight()
            if l == 0:
                ada(1)
        for i in range(N_DOWN):
            weight()
            if l == 0 and i % 2 == 0:
                ada(1)
    return out


STREAM = plan_stream()
W_AT = {i: n for n, (kind, i) in enumerate(STREAM) if kind == "w"}
A_AT = {i: n for n, (kind, i) in enumerate(STREAM) if kind == "a"}
N_WEIGHTS = len(W_AT)
assert len(STREAM) % RING == 0


def place(where, u, i, per_u, per_n):
    if isinstance(i, int):
        return where[u + per_u * i], 0
    return where[u + per_u] - per_n, per_n // RING

SMALL = {}
_at = 0
for _name, _n in [("c", 2 * KC), ("b_ada", DEPTH * 48), ("norm1", DEPTH * KC), ("norm2", DEPTH * KC), ("final", KC),
                  ("pool_scale", DEPTH * 2), ("lower", DEPTH * 4), ("hg_norm", DEPTH), ("sink", DEPTH * QH),
                  ("sel", 2), ("inv_window", 2), ("edge", 2 * 32), ("ident", P), ("ones", P), ("pair_ones", P),
                  ("rope_cos", LAT), ("rope_sin", LAT), ("pool_w", DEPTH * 2 * P)]:
    SMALL[_name] = (_at, _n)
    _at += _n
N_SMALL = _at

SEG = ((8, 0, LAT), (8 + LAT + 8, LAT, CTX))
PADW = 8 + LAT + 8 + CTX + 8
EDGES = (8, LAT, 8 + LAT + 8, LAT + 8 + CTX)
LEVELS = 7
F_ORDER = (4, 5, 0, 1, 2, 3)
B_ORDER = (5, 4, 3, 2, 1, 0)
SWAP = [(r + 16) % 32 for r in range(32)]


def quads_of(ctx):
    out = []
    for n in range(LB):
        local = [b for b in (n - 1, n, n + 1) if 0 <= b < LB]
        out += [(n, j, local + [4, 5], len(local)) for j in range(KVH)]
    if ctx:
        out += [(n, j, [4, 5], 0) for n in (4, 5) for j in range(KVH)]
    return out


def attention_steps(quads):
    steps = []
    for n in range(4 * len(quads) + 8):
        qn, c = divmod(n, 4)
        q, blocks = (qn - 1, [c - 1]) if c else (qn - 2, [3, 4])
        steps.append(((qn, c) if qn < len(quads) else None,
                      [(q, k) for k in blocks if 0 <= q < len(quads) and k < len(quads[q][2])]))
    return steps


def outputs_of(quads):
    steps, done, out = attention_steps(quads), 0, {}
    for n, (_, turned) in enumerate(steps):
        for q, k in turned:
            done += 1
            if q % 2 == 1 and k == len(quads[q][2]) - 1:
                out[n + 2] = (q // 2, quads[q][0], done)
    return out


def build_program(nc, stream, xin, small_in, masks_in, out):
    stack = ExitStack()
    with stack:
        def sb(name, shape, dt=F32):
            return stack.enter_context(nc.sbuf_tensor(name, shape, dt))

        def sem(name):
            return stack.enter_context(nc.semaphore(name))

        x = sb("x", [P, KC, TOK])
        act_hi = sb("act_hi", [P, KC, TOK], F16)
        act_lo = sb("act_lo", [P, KC, TOK], F16)
        arena = sb("arena", [P, FU * TOK + 64])
        stage = sb("stage", [P, RING, UNIT])
        w_hi = sb("w_hi", [P, RING, UNIT], F16)
        w_lo = sb("w_lo", [P, RING, UNIT], F16)
        small = sb("small", [P, N_SMALL])
        masks = sb("masks", [P, 8, P], U8)
        band = sb("band", [P, 3 * P], BF16)
        extra = sb("extra", [P, 4 * TOK])
        ada_row = sb("ada_row", [P, 512])
        rst = sb("rst", [P, TOK])
        mod = [sb(f"mod{l}", [P, 48, 2]) for l in range(DEPTH)]
        gains = sb("gains", [P, 6, KC, 2])
        silu_c = sb("silu_c", [P, KC, 32])
        sig_c = sb("sig_c", [P, KC, 2])
        nw64 = sb("nw64", [P, DEPTH * 2 * KC])
        lbt = sb("lbt", [P, DEPTH, 2, 4])
        lwork = sb("lwork", [P, 3, 4])
        hgw = sb("hgw", [P, DEPTH])
        psc = sb("psc", [P, DEPTH * 2])
        eps_t = sb("eps_t", [P, 1])
        neg_sink = sb("neg_sink", [P, DEPTH * QH])
        stat = sb("stat", [P, 2, 6, 4])
        dec = sb("dec", [P, 2, NB])

        def sm(name, i=0, n=None):
            at, size = SMALL[name]
            return small[:, at + i:at + (size if n is None else i + n)]

        ident, ones, pair_ones = sm("ident"), sm("ones"), sm("pair_ones")
        hid = arena[:, 0:FU * TOK].bitcast(F16).rearrange("p (h u t) -> p h u t", h=2, u=FU)
        h32 = arena[:, 0:KC * TOK].rearrange("p (k t) -> p k t", k=KC)

        masks32 = arena[:, 0:11 * P]

        def cutter(tensor, at, end):
            pos = [at]

            def take(n):
                assert pos[0] + n <= end, (pos[0], n, end)
                pos[0] += n
                return tensor[:, pos[0] - n:pos[0]]
            return take, pos

        take, pos = cutter(arena, 0, FU * TOK + 64)
        pa = take(2 * PADW).rearrange("p (c t) -> p c t", c=2)
        qa = take(4 * TOK).rearrange("p (c t) -> p c t", c=4)
        kpad = take(2 * TOK).rearrange("p (j t) -> p j t", j=2)
        va = take(TOK).rearrange("p (b v) -> p b v", b=NB)
        hv = take(2 * TOK).rearrange("p (c b v) -> p c b v", c=2, b=NB)
        qs = take(2 * TOK).rearrange("p (c t) -> p c t", c=2)
        kk = take(4 * TOK).rearrange("p (d c t) -> p d c t", d=2, c=2)
        cum_f = take(2 * TOK).rearrange("p (c b t) -> p c b t", c=2, b=NB)
        cum_b = take(2 * NB * 129).rearrange("p (c b t) -> p c b t", c=2, b=NB)
        gate = take(2 * TOK).rearrange("p (c t) -> p c t", c=2)
        shared = pos[0]
        gbuf = take(4 * TOK).rearrange("p (g t) -> p g t", g=4)
        sgt = take(2 * TOK).rearrange("p (s t) -> p s t", s=2)
        rot = take(2 * LAT).rearrange("p (s t) -> p s t", s=2)
        pos[0] = shared
        prob = take(8 * 640).rearrange("p (s c k) -> p s c k", s=2, c=4)
        prob_t = take(2 * 512).rearrange("p (s n) -> p s n", s=2)
        pos[0] = shared
        amat = take(2 * TOK).rearrange("p (b h t) -> p b h t", b=NB, h=2)
        level_at = pos[0]
        levels = []
        for pos[0] in (level_at, 2 * PADW):
            levels.append((take(2 * TOK).rearrange("p (d t) -> p d t", d=2), take(TOK), take(TOK), take(TOK),
                           take(2 * TOK).rearrange("p (h t) -> p h t", h=2)))
        diff, ek, eq, km, qm = levels[0]
        kt = arena[:, 0:2 * TOK].rearrange("p (d b k) -> p d b k", d=2, b=NB)
        take, pos = cutter(extra, 0, 4 * TOK)
        pool_a, pool_b = take(PADW), take(PADW)
        pos[0] = 0
        state = take(2 * NB * P).rearrange("p (d b v) -> p d b v", d=2, b=NB)
        qi = take(2 * TOK).rearrange("p (d t) -> p d t", d=2)
        pos[0] = 0
        relu = take(2 * TOK).rearrange("p (s t) -> p s t", s=2)
        hid32 = take(2 * TOK).rearrange("p (s t) -> p s t", s=2)
        sq = relu
        sq_sum = hid32[:, 1, :]

        ps = stack.enter_context(nc.psum_tensor("ps", [P, 8 * 512], F32))

        def bank(b, n=512, at=0):
            return ps[:, b * 512 + at:b * 512 + at + n]

        stage_full = [sem(f"stage_full{i}") for i in range(RING)]
        stage_taken = [sem(f"stage_taken{i}") for i in range(RING)]
        hi_ready = sem("hi_ready")
        unit_used = sem("unit_used")
        tile_free = [sem("tile_free0"), sem("tile_free1")]
        small_here, x_here, masks_here, masks_ready = sem("small_here"), sem("x_here"), sem("masks_here"), sem("masks_ready")
        setup_v, setup_a, setup_done = sem("setup_v"), sem("setup_a"), sem("setup_done")
        ada_copied, ada_cols, mod_ready = sem("ada_copied"), sem("ada_cols"), sem("mod_ready")
        sq_ready, sq_added, sq_used = sem("sq_ready"), sem("sq_added"), sem("sq_used")
        rst_log, rst_ready = sem("rst_log"), sem("rst_ready")
        h_scaled, h32_ready, hhi_ready, act_ready = sem("h_scaled"), sem("h32_ready"), sem("hhi_ready"), sem("act_ready")
        hid32_ready, hidhi_ready, hid_ready = sem("hid32_ready"), sem("hidhi_ready"), sem("hid_ready")
        out_ready, out_sent = sem("out_ready"), sem("out_sent")
        dve_chain, pool_chain = sem("dve_chain"), sem("pool_chain")
        names = ("zeroed pool_diff pool_mm pool_y pool_hi pool_lo state_zero sig f_ready k_ready g_ready roped cum_ready "
                 "scores negmax exped esink_in esink rinv normed normed_v pt_done pt_copied pv_done o_hi o_lo "
                 "d_inter e_inter w_inter kt_tr kt_copied p_done st_half st_ready d_ready e_ready m_ready a_done a_copied "
                 "o_done osq oss orst_log orst o_scaled oy oy_hi oy_lo").split()
        S = [{n: sem(f"{n}_{l}") for n in names} for l in range(DEPTH)]
        block = stack.enter_context(nc.Block())

        def tokens(l):
            return TOK if l < DEPTH - 1 else LAT

        def parts(t):
            return [(0, LAT)] + ([(LAT, CTX)] if t == TOK else [])

        def in_tokens(l, name):
            return TOK if l < DEPTH - 1 or name in CTX_NEEDED_LAST else LAT

        W_IN = [l * (N_IN + N_OUT + N_UP + N_DOWN) for l in range(DEPTH)]
        W_OUT = [w + N_IN for w in W_IN]
        W_UP = [w + N_OUT for w in W_OUT]
        W_DOWN = [w + N_UP for w in W_UP]
        G_IN = [l * (N_IN + N_OUT + N_UP + KC) for l in range(DEPTH)]
        G_OUT = [g + N_IN for g in G_IN]
        G_UP = [g + N_OUT for g in G_OUT]
        G_DOWN = [g + N_UP for g in G_UP]
        NORMS = 2 * DEPTH + 1

        def freed(eng, g, i=0):
            eng.wait_ge(tile_free[g % 2], 2 * (g // 2 + 1) + i)

        def norm_tokens(idx):
            return LAT if idx == NORMS - 1 or idx == 2 * DEPTH - 1 else TOK

        @block.sync
        def _(sp):
            sp.dma_start(small[:, :], small_in).then_inc(small_here, 16)
            for n in range(RING):
                sp.dma_start(stage[:, n, :], stream[n]).then_inc(stage_full[n], 16)
            with sp.Fori(1, len(STREAM) // RING) as i:
                for s in range(RING):
                    sp.wait_ge(stage_taken[s], i)
                    sp.dma_start(stage[:, s, :], stream[RING * i + s]).then_inc(stage_full[s], 16)
            for k in range(KC):
                sp.wait_ge(out_ready, k + 1)
                sp.dma_start(out[k * P:(k + 1) * P, :], h32[:, k, 0:LAT]).then_inc(out_sent, 16)
            sp.wait_ge(out_sent, 16 * KC)

        @block.scalar
        def _(act):
            act.dma_start(x[:, :, :], xin.rearrange("(k p) t -> p k t", p=P)).then_inc(x_here, 16)
            act.dma_start(masks32, masks_in).then_inc(masks_here, 16)

            def split_hi(w, i=0, per_w=0, per_n=0):
                n, more = place(W_AT, w, i, per_w, per_n)
                act.wait_ge(stage_full[n % RING], 16 * (n // RING + 1) + 16 * more * i)
                if w >= RING:
                    act.wait_ge(unit_used, w - RING + 1 + per_w * i)
                act.activation(w_hi[:, w % RING, :], stage[:, n % RING, :], ACT.Copy, scale=W_SCALE).then_inc(hi_ready, 1)

            def ada_copy(b, i=0, per_n=0):
                n, more = place(A_AT, 4 * b + 3, i, 4, per_n)
                act.wait_ge(stage_taken[n % RING], n // RING + 1 + more * i)
                if b > 0:
                    act.wait_ge(ada_cols, b + i)
                act.activation(ada_row[:, :], bank(6), ACT.Copy).then_inc(ada_copied, 1)

            act.wait_ge(small_here, 16)
            act.activation(sig_c[:, :, :], sm("c").rearrange("p (k v) -> p k v", v=2), ACT.Sigmoid).then_inc(setup_a, 1)
            act.wait_ge(setup_v, 1)
            act.activation(lwork[:, 0:2, :], lwork[:, 0:2, :], ACT.Exp).then_inc(setup_a, 1)

            logs = [0]

            def square(idx, k, buf):
                T = norm_tokens(idx)
                if idx > 0 or k >= 2:
                    act.wait_ge(sq_added, KC * idx - 1 + k)
                xs = x[:, k, 0:T] if isinstance(k, int) else x[:, bass.ds(k, 1), 0:T]
                dst = sq[:, buf, 0:T] if isinstance(k, int) else sq[:, buf:buf + 1, 0:T]
                act.activation(dst, xs, ACT.Square).then_inc(sq_ready, 1)

            def inverse_rms(idx):
                act.wait_ge(sq_used, idx + 1)
                T = norm_tokens(idx)
                for n, (t0, t) in enumerate(parts(T)):
                    act.activation(rst[:, t0:t0 + t], bank(4 + n, t), ACT.Ln, bias=eps_t[:, 0:1], scale=1.0 / D).then_inc(rst_log, 1)
                    logs[0] += 1
                act.wait_ge(rst_log, logs[0])
                act.activation(rst[:, 0:T], rst[:, 0:T], ACT.Exp, scale=-0.5).then_inc(rst_ready, 1)

            def split_norm(idx):
                T = norm_tokens(idx)
                for k in range(KC):
                    act.wait_ge(h32_ready, idx * KC + k + 1)
                    act.activation(act_hi[:, k, 0:T], h32[:, k, 0:T], ACT.Copy).then_inc(hhi_ready, 1)

            act.wait_ge(setup_done, 1)
            act.wait_ge(x_here, 16)
            for k in range(KC):
                square(0, k, k % 2)
            for b in range(4):
                if b == 3:
                    inverse_rms(0)
                ada_copy(b)
            for w in range(AHEAD):
                split_hi(w)

            for l in range(DEPTH):
                s = S[l]
                T = tokens(l)
                pp = parts(T)
                if l > 0:
                    inverse_rms(2 * l)
                split_norm(2 * l)

                for i, (name, c) in enumerate(IN_ORDER):
                    g = G_IN[l] + i
                    split_hi(W_IN[l] + i + AHEAD)
                    if l == 0 and i % 2 == 0 and i > 0:
                        ada_copy(3 + i // 2)
                    pi = parts(in_tokens(l, name))
                    inc = 2 // len(pi)
                    if i == 0:
                        act.wait_ge(s["zeroed"], 1)
                    if name == "gh":
                        freed(act, G_IN[l] + IN_ORDER.index(("qh", c)))
                    act.wait_ge(unit_used, W_IN[l] + i + 1)
                    for n, (t0, t) in enumerate(pi):
                        src = bank(g % 2 + 2 * n, t)
                        if name in ("qh", "gh"):
                            act.activation(sgt[:, c, t0:t0 + t], src, ACT.Sigmoid, scale=UNSCALE).then_inc(s["sig"], 1)
                            continue
                        if name == "pool":
                            ins = act.activation(pa[:, c, SEG[n][0]:SEG[n][0] + t], src, ACT.Copy, scale=UNSCALE)
                        elif name in ("ff", "fb"):
                            ins = act.activation(gbuf[:, 2 * (name == "fb") + c, t0:t0 + t], src, ACT.Sigmoid, scale=UNSCALE)
                        elif name == "ih":
                            ins = act.activation(hv[:, c, t0 // P:(t0 + t) // P, :], src.rearrange("p (b v) -> p b v", v=P), ACT.Copy, scale=UNSCALE)
                        elif name == "va":
                            ins = act.activation(va[:, t0 // P:(t0 + t) // P, :], src.rearrange("p (b v) -> p b v", v=P), ACT.Copy, scale=UNSCALE)
                        elif name == "k":
                            for j in range(KVH):
                                h = slice(HD * j, HD * j + HD)
                                ins = act.activation(kpad[h, j, t0:t0 + t], ps[h, (g % 2 + 2 * n) * 512:(g % 2 + 2 * n) * 512 + t], ACT.Copy, scale=UNSCALE)
                        else:
                            ins = act.activation(qa[:, c, t0:t0 + t], src, ACT.Copy, scale=UNSCALE * HD ** -0.5)
                        ins.then_inc(tile_free[g % 2], inc)
                act.wait_ge(s["k_ready"], 4)
                for gi in range(4):
                    act.activation(gbuf[:, gi, :], gbuf[:, gi, :], ACT.Ln).then_inc(s["g_ready"], 1)
                for c in range(2):
                    act.wait_ge(s["pool_mm"], c + 1)
                    for n, (t0, t) in enumerate(pp):
                        act.activation(pa[:, c, t0:t0 + t], bank(2 * c + n, t), ACT.Copy, scale=psc[:, 2 * l + c:2 * l + c + 1]).then_inc(s["pool_y"], 1)
                    act.wait_ge(s["pool_y"], (c + 1) * len(pp))
                    act.activation(act_hi[:, c, 0:T], pa[:, c, 0:T], ACT.Copy).then_inc(s["pool_hi"], 1)

                quads = quads_of(l < DEPTH - 1)
                key_blocks = [len(q[2]) for q in quads]
                act.wait_ge(s["cum_ready"], 4)
                freed(act, G_IN[l] + N_IN - 2)
                freed(act, G_IN[l] + N_IN - 1)
                pt = 0
                outputs = outputs_of(quads)
                for step, (scored, turned) in enumerate(attention_steps(quads)):
                    for _ in turned:
                        act.wait_ge(s["pt_done"], pt + 1)
                        if pt >= 2:
                            act.wait_ge(s["pv_done"], pt - 1)
                        act.activation(prob_t[:, pt % 2, :], bank(4 + pt % 2), ACT.Copy).then_inc(s["pt_copied"], 1)
                        pt += 1
                    if scored:
                        qn, c = scored
                        n, j, keys, nl = quads[qn]
                        st = stat[:, qn % 2]
                        if qn >= 2 and c == 0:
                            act.wait_ge(s["pt_done"], sum(key_blocks[:qn - 1]))
                        it = 4 * qn + c
                        act.wait_ge(s["negmax"], it + 1)
                        w_ = P * len(keys)
                        b0 = 2 * (it % 2) * 512 + 512 - P * nl
                        act.activation(prob[:, qn % 2, c, 0:w_], ps[:, b0:b0 + w_], ACT.Exp,
                                       bias=st[:, 0, c:c + 1], accum_out=st[:, 2, c:c + 1]).then_inc(s["exped"], 1)
                        if c == 3:
                            act.wait_ge(s["esink_in"], qn + 1)
                            act.activation(st[:, 3, :], st[:, 1, :], ACT.Exp).then_inc(s["esink"], 1)
                    if step in outputs:
                        _, n, products = outputs[step]
                        act.wait_ge(s["pv_done"], products)
                        act.activation(act_hi[:, 2:6, n * P:n * P + P], bank(6 + n % 2).rearrange("p (c t) -> p c t", c=4),
                                       ACT.Copy).then_inc(s["o_hi"], 1)

                for c in range(2):
                    act.wait_ge(s["d_inter"], 2 * (c + 1))
                    if c == 1:
                        act.wait_ge(s["oy"], 1)
                    act.activation(ek, diff[:, 0, :], ACT.Exp).then_inc(s["e_inter"], 1)
                    act.activation(eq.rearrange("p (b t) -> p b t", b=NB), cum_b[:, c, :, 0:P], ACT.Exp).then_inc(s["e_inter"], 1)
                    act.activation(km[:, 0:T].rearrange("p (b t) -> p b t", t=P), cum_f[:, c, 0:T // P, :], ACT.Exp).then_inc(s["e_inter"], 1)
                    act.activation(diff[:, 1, 0:T], diff[:, 1, 0:T], ACT.Exp).then_inc(s["e_inter"], 1)
                    act.activation(dec[:, 0, :], cum_f[:, c, :, P - 1], ACT.Exp).then_inc(s["e_inter"], 1)
                    act.activation(dec[:, 1, :], cum_b[:, c, :, P], ACT.Exp).then_inc(s["e_inter"], 1)
                    if c == 0:
                        act.wait_ge(s["state_zero"], 1)
                    for d in range(2):
                        act.wait_ge(s["kt_tr"], 2 * c + d + 1)
                        act.activation(kt[:, d].rearrange("p b k -> p (b k)"), ps[:, 1024 * d:1024 * d + TOK], ACT.Copy).then_inc(s["kt_copied"], 1)
                    for v in range(LEVELS):
                        h = P >> (v + 1)
                        m = c * LEVELS + v
                        act.wait_ge(s["d_ready"], 2 * (m + 1))
                        if v == 1:
                            act.wait_ge(s["w_inter"], 4 * (c + 1))
                        elif c > 0 or v > 1:
                            act.wait_ge(s["m_ready"], 4 * (c * (LEVELS + 1) + v - 1))
                        diff_v, ek_v, eq_v = levels[(v + 1) % 2][:3]
                        halves = [b.rearrange("p (b s t) -> p b s t", s=2, t=h) for b in (diff_v[:, 0, 0:T], diff_v[:, 1, 0:T], ek_v[:, 0:T], eq_v[:, 0:T])]
                        df, db, ekv, eqv = halves
                        act.activation(ekv[:, :, 0], df[:, :, 0], ACT.Exp, scale=-1.0).then_inc(s["e_ready"], 1)
                        act.activation(ekv[:, :, 1], db[:, :, 1], ACT.Exp).then_inc(s["e_ready"], 1)
                        act.activation(eqv[:, :, 0], db[:, :, 0], ACT.Exp, scale=-1.0).then_inc(s["e_ready"], 1)
                        act.activation(eqv[:, :, 1], df[:, :, 1], ACT.Exp).then_inc(s["e_ready"], 1)
                    act.wait_ge(s["o_done"], c + 1)
                    act.wait_ge(s["m_ready"], 4 * (LEVELS + 1) * (c + 1))
                    for n, (t0, t) in enumerate(pp):
                        act.activation(ek[:, t0:t0 + t], bank(6 + n, t), ACT.Square).then_inc(s["osq"], 1)
                    act.wait_ge(s["oss"], c + 1)
                    for n, (t0, t) in enumerate(pp):
                        act.activation(eq[:, t0:t0 + t], bank(n, t), ACT.Ln, bias=eps_t[:, 0:1], scale=1.0 / HD).then_inc(s["orst_log"], 1)
                    act.wait_ge(s["orst_log"], (c + 1) * len(pp))
                    act.activation(eq[:, 0:T], eq[:, 0:T], ACT.Exp, scale=-0.5).then_inc(s["orst"], 1)
                    act.wait_ge(s["oy"], c + 1)
                    act.activation(act_hi[:, 6 + c, 0:T], diff[:, 1, 0:T], ACT.Copy).then_inc(s["oy_hi"], 1)

                for i in range(N_OUT):
                    split_hi(W_OUT[l] + i + AHEAD)
                    if i > 0:
                        freed(act, G_OUT[l] + i - 1)
                        square(2 * l + 1, i - 1, (i - 1) % 2)
                freed(act, G_OUT[l] + N_OUT - 1)
                square(2 * l + 1, KC - 1, 1)
                inverse_rms(2 * l + 1)
                split_norm(2 * l + 1)

                def up(i):
                    for j in range(4):
                        split_hi(W_UP[l] + j + AHEAD, i, 4, 8 if l == 0 else 4)
                        if l == 0 and j == 0 and not (isinstance(i, int) and i == 0):
                            ada_copy(ADA_BLOCKS - 1, i, 8)
                        g = G_UP[l] + j
                        u = 4 * i + j
                        act.wait_ge(unit_used, W_UP[l] + j + 1 + 4 * i)
                        if l > 0 or j >= 2 or not isinstance(i, int):
                            act.wait_ge(hid32_ready, l * N_UP - 1 + j + 4 * i)
                        for n, (t0, t) in enumerate(pp):
                            act.activation(relu[:, g % 2, t0:t0 + t], bank(g % 2 + 2 * n, t), ACT.Relu, scale=UNSCALE).then_inc(tile_free[g % 2], 2 // len(pp))
                        act.wait_ge(hid32_ready, l * N_UP + 1 + j + 4 * i)
                        act.activation(hid[:, 0, bass.ds(u, 1), 0:T], hid32[:, j % 2, 0:T].unsqueeze(1), ACT.Copy).then_inc(hidhi_ready, 1)

                def down(i, last=False):
                    for j in range(8):
                        if not (last and j >= 8 - AHEAD):
                            split_hi(W_DOWN[l] + j + AHEAD, i, 8, 12 if l == 0 else 8)
                        if l == 0 and j == 0:
                            ada_copy(ADA_BLOCKS + N_UP // 4 - 1, i, 12)
                        if j % 4 == 0:
                            if j == 4:
                                freed(act, G_DOWN[l], 2 * i)
                                square(2 * l + 2, 2 * i, 0)
                            elif not isinstance(i, int) or i > 0:
                                freed(act, G_DOWN[l] + 1, 2 * i - 2)
                                square(2 * l + 2, 2 * i - 1, 1)

                up(0)
                with act.Fori(1, N_UP // 4) as i:
                    up(i)
                down(0)
                with act.Fori(1, N_DOWN // 8 - 1) as i:
                    down(i)
                down(N_DOWN // 8 - 1, l == DEPTH - 1)
                if l == 0:
                    ada_copy(2 * ADA_BLOCKS - 1)
                freed(act, G_DOWN[l] + KC - 1)
                square(2 * l + 2, KC - 1, 1)
            inverse_rms(NORMS - 1)

        @block.vector
        def _(dve):
            links = [0]

            def link(ins):
                links[0] += 1
                ins.then_inc(dve_chain, 1)
                dve.wait_ge(dve_chain, links[0])

            def split_lo(w, i=0, per_w=0):
                n = W_AT[w] if isinstance(i, int) and per_w == 0 else place(W_AT, w, i, per_w, RING)[0]
                dve.wait_ge(hi_ready, w + 1 + per_w * i)
                dve.scalar_tensor_tensor(out=w_lo[:, w % RING, :], in0=stage[:, n % RING, :], scalar=W_SCALE,
                                         in1=w_hi[:, w % RING, :], op0=ALU.mult, op1=ALU.subtract).then_inc(stage_taken[n % RING], 1)

            def ada_mod(l, b, i=0):
                dve.wait_ge(ada_cols, ADA_BLOCKS * l + b + 1 + i)
                at = SMALL["b_ada"][0] + 48 * l + 4 * b + 4 * i
                dve.tensor_tensor(mod[l][:, bass.ds(4 * b + 4 * i, 4), :], bank(7, 8).rearrange("p (k v) -> p k v", v=2),
                                  small[:, bass.ds(at, 4)].unsqueeze(2).broadcast_to([P, 4, 2]), ALU.add).then_inc(mod_ready, 1)

            link(dve.memset(silu_c[:, :, :], 0.0))
            link(dve.memset(eps_t[:, :], EPS))
            link(dve.memset(lbt[:, 0, 0, :], 0.0))
            link(dve.memset(lbt[:, 0, 1, :], 1.0))
            dve.wait_ge(small_here, 16)
            lo0, lo1 = sm("lower", 0, 4), sm("lower", 4, 4)
            link(dve.tensor_tensor(lwork[:, 2, :], lo0, lo1, ALU.max))
            link(dve.tensor_tensor(lwork[:, 0, :], lo0, lwork[:, 2, :], ALU.subtract))
            dve.tensor_tensor(lwork[:, 1, :], lo1, lwork[:, 2, :], ALU.subtract).then_inc(setup_v, 1)
            dve.wait_ge(setup_a, 2)
            dve.tensor_tensor(silu_c[:, :, 0:2], sm("c").rearrange("p (k v) -> p k v", v=2), sig_c[:, :, :], ALU.mult).then_inc(setup_done, 1)
            link(dve.tensor_tensor(lwork[:, 0, :], lwork[:, 0, :], lwork[:, 1, :], ALU.add))
            link(dve.reciprocal(lwork[:, 2, :], lwork[:, 0, :]))
            link(dve.tensor_tensor(lbt[:, 1, 0, :], lwork[:, 1, :], lwork[:, 2, :], ALU.mult))
            link(dve.tensor_scalar(lbt[:, 1, 1, :], lbt[:, 1, 0, :], -1.0, 1.0, ALU.mult, ALU.add))
            link(dve.tensor_scalar(nw64[:, :], small[:, SMALL["norm1"][0]:SMALL["norm1"][0] + 4 * KC], A_SCALE, None, ALU.mult))
            link(dve.tensor_scalar(hgw[:, :], sm("hg_norm"), A_SCALE * UNSCALE, None, ALU.mult))
            link(dve.tensor_scalar(neg_sink[:, :], sm("sink"), -1.0, None, ALU.mult))
            dve.tensor_scalar(psc[:, :], sm("pool_scale"), A_SCALE, None, ALU.mult).then_inc(setup_done, 1)
            dve.wait_ge(masks_here, 16)
            dve.tensor_copy(masks[:, :, :], masks32[:, 0:8 * P].rearrange("p (v t) -> p v t", v=8)).then_inc(masks_ready, 1)
            dve.tensor_copy(band[:, :], masks32[:, 8 * P:11 * P]).then_inc(masks_ready, 1)
            dve.wait_ge(masks_ready, 2)
            for b in range(4):
                ada_mod(0, b)
            for w in range(AHEAD):
                split_lo(w)

            def make_gains(l, half):
                o = 24 * half
                dve.wait_ge(mod_ready, ADA_BLOCKS * (l + half) + (0 if half else 4))
                for v in range(2):
                    link(dve.scalar_tensor_tensor(out=gains[:, 3 * half, :, v], in0=mod[l][:, o + 8:o + 16, v], scalar=1.0,
                                                  in1=nw64[:, 16 * half + 8 * l:16 * half + 8 * l + KC], op0=ALU.add, op1=ALU.mult))
                link(dve.tensor_scalar(gains[:, 3 * half + 1, :, :], mod[l][:, o:o + 8, :], A_SCALE, None, ALU.mult))

            def make_gate(l, half):
                o = 24 * half + 16
                dve.wait_ge(mod_ready, ADA_BLOCKS * (l + 1))
                link(dve.tensor_scalar(gains[:, 3 * half + 2, :, :], mod[l][:, o:o + 8, :], UNSCALE2 if half else UNSCALE, None, ALU.mult))

            def norm(idx):
                T = norm_tokens(idx)
                half = idx % 2
                dve.wait_ge(rst_ready, idx + 1)
                if idx == NORMS - 1:
                    for k in range(KC):
                        dve.scalar_tensor_tensor(out=h32[:, k, 0:T], in0=x[:, k, 0:T], scalar=sm("final", k, 1), in1=rst[:, 0:T],
                                                 op0=ALU.mult, op1=ALU.mult).then_inc(out_ready, 1)
                    return
                for k in range(KC + 1):
                    if k < KC:
                        dve.tensor_tensor(h32[:, k, 0:T], x[:, k, 0:T], rst[:, 0:T], ALU.mult).then_inc(h_scaled, 1)
                    if k > 0:
                        dve.wait_ge(h_scaled, KC * idx + k)
                        for n, (t0, t) in enumerate(parts(T)):
                            ins = dve.tensor_scalar(h32[:, k - 1, t0:t0 + t], h32[:, k - 1, t0:t0 + t], gains[:, 3 * half, k - 1, n:n + 1],
                                                    gains[:, 3 * half + 1, k - 1, n:n + 1], ALU.mult, ALU.add)
                            if t0 + t == T:
                                ins.then_inc(h32_ready, 1)
                            else:
                                links[0] += 1
                                ins.then_inc(dve_chain, 1)

            for l in range(DEPTH):
                s = S[l]
                T = tokens(l)
                pp = parts(T)
                make_gains(l, 0)
                norm(2 * l)
                sigs = ropes = 0
                for i, (name, c) in enumerate(IN_ORDER):
                    g = G_IN[l] + i
                    split_lo(W_IN[l] + i + AHEAD)
                    pi = parts(in_tokens(l, name))
                    if name in ("ff", "fb"):
                        gi = 2 * (name == "fb") + c
                        freed(dve, g)
                        dve.tensor_scalar(gbuf[:, gi, :], gbuf[:, gi, :], lbt[:, l, 1, gi:gi + 1], lbt[:, l, 0, gi:gi + 1],
                                          ALU.mult, ALU.add).then_inc(s["f_ready"], 1)
                        dve.wait_ge(s["f_ready"], gi + 1)
                        dve.tensor_scalar(kk[:, gi // 2, gi % 2, :], gbuf[:, gi, :], -1.0, 1.0, ALU.mult, ALU.add).then_inc(s["k_ready"], 1)
                    elif name in ("qh", "gh"):
                        for n, (t0, t) in enumerate(pi):
                            sigs += 1
                            dve.wait_ge(s["sig"], sigs)
                            dst, scale = (qs, UNSCALE) if name == "qh" else (gate, hgw[:, l:l + 1])
                            dve.scalar_tensor_tensor(out=dst[:, c, t0:t0 + t], in0=bank(g % 2 + 2 * n, t), scalar=scale, in1=sgt[:, c, t0:t0 + t],
                                                     op0=ALU.mult, op1=ALU.mult).then_inc(tile_free[g % 2], 2 // len(pi))
                    elif name in ("k", "q"):
                        freed(dve, g)
                        if name == "q":
                            jobs = [(slice(0, P), c)]
                        else:
                            jobs = [(slice(0, HD), 0), (slice(HD, P), 1)]
                        for r, jc in jobs:
                            v = (qa if name == "q" else kpad)[r, jc, 0:LAT]
                            cos, sin = (small[r, SMALL[n][0]:SMALL[n][0] + LAT] for n in ("rope_cos", "rope_sin"))
                            link(dve.stream_shuffle(rot[r, 0, :], v, SWAP))
                            link(dve.tensor_tensor(rot[r, 0, :], rot[r, 0, :], sin, ALU.mult))
                            link(dve.tensor_tensor(rot[r, 1, :], v, cos, ALU.mult))
                            dve.tensor_tensor(v, rot[r, 0, :], rot[r, 1, :], ALU.add).then_inc(s["roped"], 1)
                            ropes += 1
                            dve.wait_ge(s["roped"], ropes)
                    if l == 0 and i % 2 == 0 and i > 0:
                        ada_mod(0, 3 + i // 2)
                make_gate(l, 0)
                for gi in range(4):
                    dve.wait_ge(s["g_ready"], gi + 1)
                    for b in range(NB):
                        dst = cum_f[:, gi % 2, b, :] if gi < 2 else cum_b[:, gi % 2, b, 1:P + 1]
                        ins = dve.tensor_tensor_scan(dst, ones, gbuf[:, gi, b * P:(b + 1) * P], 0.0, ALU.mult, ALU.add)
                        if b < NB - 1:
                            links[0] += 1
                            ins.then_inc(dve_chain, 1)
                    ins.then_inc(s["cum_ready"], 1)
                dve.wait_ge(dve_chain, links[0])
                dve.wait_ge(s["cum_ready"], 4)
                quads = quads_of(l < DEPTH - 1)
                outputs = outputs_of(quads)
                for step, (scored, turned) in enumerate(attention_steps(quads)):
                    last = step // 4 - 1
                    sums = step % 4 == 0 and 0 <= last < len(quads)
                    if sums:
                        st = stat[:, last % 2]
                        dve.wait_ge(s["esink"], last + 1)
                        link(dve.tensor_tensor(st[:, 4, :], st[:, 2, :], st[:, 3, :], ALU.add))
                        dve.reciprocal(st[:, 5, :], st[:, 4, :]).then_inc(s["rinv"], 1)
                    if scored:
                        qn, c = scored
                        n, j, keys, nl = quads[qn]
                        st = stat[:, qn % 2]
                        at = QH * l + 4 * j
                        if qn >= 2 and c == 0:
                            dve.wait_ge(s["normed"], 2 * (qn - 1))
                            dve.wait_ge(s["normed_v"], 2 * (qn - 1))
                        it = 4 * qn + c
                        dve.wait_ge(s["scores"], it + 1)
                        w_ = P * len(keys)
                        b0 = 2 * (it % 2) * 512 + 512 - P * nl
                        link(dve.tensor_reduce(st[:, 4, c:c + 1], ps[:, b0:b0 + w_], AX_X, ALU.max, negate=True))
                        dve.tensor_tensor(st[:, 0, c:c + 1], st[:, 4, c:c + 1], neg_sink[:, at + c:at + c + 1], ALU.min).then_inc(s["negmax"], 1)
                        if c == 3:
                            dve.wait_ge(s["negmax"], 4 * qn + 4)
                            dve.tensor_tensor(st[:, 1, :], st[:, 0, :], sm("sink", at, 4), ALU.add).then_inc(s["esink_in"], 1)
                    if sums:
                        dve.wait_ge(s["rinv"], last + 1)
                        for c in (2, 3):
                            v = prob[:, last % 2, c, 0:P * len(quads[last][2])]
                            dve.tensor_scalar(v, v, stat[:, last % 2, 5, c:c + 1], A_SCALE, ALU.mult, ALU.mult).then_inc(s["normed_v"], 1)
                    if step in outputs:
                        low, n, _ = outputs[step]
                        dve.wait_ge(s["o_hi"], low + 1)
                        dve.tensor_tensor(act_lo[:, 2:6, n * P:n * P + P], bank(6 + n % 2).rearrange("p (c t) -> p c t", c=4),
                                          act_hi[:, 2:6, n * P:n * P + P], ALU.subtract).then_inc(s["o_lo"], 1)

                nsp = T // P
                dve.wait_ge(s["pv_done"], sum(len(q[2]) for q in quads))
                for c in range(2):
                    if c == 1:
                        dve.wait_ge(s["oy_lo"], 1)
                    kf, kb = kk[:, 0, c, :], kk[:, 1, c, :]
                    blocks = [diff[:, d, :].rearrange("p (b t) -> p b t", b=NB) for d in range(2)]
                    dve.tensor_tensor(blocks[0], cum_f[:, c, :, P - 1:P].broadcast_to([P, NB, P]), cum_f[:, c], ALU.subtract).then_inc(s["d_inter"], 1)
                    dve.tensor_tensor(blocks[1], cum_b[:, c, :, P:P + 1].broadcast_to([P, NB, P]), cum_b[:, c, :, 0:P], ALU.subtract).then_inc(s["d_inter"], 1)
                    dve.wait_ge(s["e_inter"], 6 * (c + 1))
                    dve.tensor_tensor(ek, ek, kf, ALU.mult).then_inc(s["w_inter"], 1)
                    dve.tensor_tensor(eq, eq, kb, ALU.mult).then_inc(s["w_inter"], 1)
                    if c == 0:
                        dve.wait_ge(s["state_zero"], 1)
                    dve.tensor_tensor(qi[:, 0, 0:T], km[:, 0:T], qs[:, c, 0:T], ALU.mult).then_inc(s["w_inter"], 1)
                    dve.tensor_tensor(qi[:, 1, 0:T], diff[:, 1, 0:T], qs[:, c, 0:T], ALU.mult).then_inc(s["w_inter"], 1)
                    dve.wait_ge(s["kt_tr"], 2 * (c + 1))
                    dve.wait_ge(s["p_done"], c + 1)
                    for d, order in enumerate((F_ORDER, B_ORDER)):
                        for m in range(1, NB):
                            prev, cur = order[m - 1], order[m]
                            at = (4 + 2 * d) * 512 + P * (m - 1)
                            for h in range(2):
                                r = slice(HD * h, HD * h + HD)
                                src = ps[r, at + HD * h:at + HD * h + HD]
                                if m == 1:
                                    ins = dve.tensor_copy(state[r, d, cur, r], src)
                                else:
                                    ins = dve.scalar_tensor_tensor(out=state[r, d, cur, r], in0=state[r, d, prev, r], scalar=dec[r, d, prev:prev + 1],
                                                                   in1=src, op0=ALU.mult, op1=ALU.add)
                                ins.then_inc(s["st_ready" if h else "st_half"], 1)
                            done = c * 10 + d * 5 + m
                            dve.wait_ge(s["st_half"], done)
                            dve.wait_ge(s["st_ready"], done)

                    for v in range(LEVELS + 2):
                        m = c * (LEVELS + 1) + v
                        km_v, qm_v = levels[(v + 1) % 2][3:]
                        if v <= LEVELS and (v >= 2 or c > 0 and v == 0):
                            dve.wait_ge(s["a_done"], m - 1)
                        if v < LEVELS:
                            h = P >> (v + 1)
                            dve.wait_ge(s["e_ready"], 4 * (c * LEVELS + v + 1))
                            for side, kx in ((0, kf), (1, kb)):
                                o, e_, k_ = (b.rearrange("p (b s t) -> p b s t", s=2, t=h)[:, :, side] for b in (km_v[:, 0:T], levels[(v + 1) % 2][1][:, 0:T], kx[:, 0:T]))
                                dve.tensor_tensor(o, e_, k_, ALU.mult).then_inc(s["m_ready"], 1)
                            for hh in range(2):
                                r = slice(HD * hh, HD * hh + HD)
                                dve.tensor_tensor(qm_v[r, hh, 0:T], qs[r, c, 0:T], levels[(v + 1) % 2][2][r, 0:T], ALU.mult).then_inc(s["m_ready"], 1)
                        elif v == LEVELS:
                            dve.tensor_tensor(km_v[:, 0:T], kf[:, 0:T], kb[:, 0:T], ALU.add).then_inc(s["m_ready"], 2)
                            for hh in range(2):
                                r = slice(HD * hh, HD * hh + HD)
                                dve.tensor_copy(qm_v[r, hh, 0:T], qs[r, c, 0:T]).then_inc(s["m_ready"], 1)
                        if v >= 1:
                            dve.wait_ge(s["a_done"], m)
                            if m > 1:
                                dve.wait_ge(s["a_copied"], m - 1)
                            src = bank(3 * ((v - 1) % 2), 2 * T).rearrange("p (n t) -> p n t", t=P)
                            dst = amat[:, 0:nsp].rearrange("p b h t -> p (b h) t")
                            if v == 1:
                                ins = dve.tensor_copy(dst, src)
                            else:
                                ins = dve.copy_predicated(dst, masks[:, v - 1:v, :].broadcast_to([P, 2 * nsp, P]), src)
                            ins.then_inc(s["a_copied"], 1)
                    dve.wait_ge(s["orst"], c + 1)
                    for n, (t0, t) in enumerate(pp):
                        dve.tensor_tensor(diff[:, 0, t0:t0 + t], bank(6 + n, t), eq[:, t0:t0 + t], ALU.mult).then_inc(s["o_scaled"], 1)
                    dve.wait_ge(s["o_scaled"], (c + 1) * len(pp))
                    dve.tensor_tensor(diff[:, 1, 0:T], diff[:, 0, 0:T], gate[:, c, 0:T], ALU.mult).then_inc(s["oy"], 1)
                    dve.wait_ge(s["oy_hi"], c + 1)
                    dve.tensor_tensor(act_lo[:, 6 + c, 0:T], diff[:, 1, 0:T], act_hi[:, 6 + c, 0:T], ALU.subtract).then_inc(s["oy_lo"], 1)

                for i in range(N_OUT):
                    split_lo(W_OUT[l] + i + AHEAD)
                    g = G_OUT[l] + i
                    dve.wait_ge(unit_used, W_OUT[l] + i + 1)
                    for n, (t0, t) in enumerate(pp):
                        dve.scalar_tensor_tensor(out=x[:, i, t0:t0 + t], in0=bank(g % 2 + 2 * n, t), scalar=gains[:, 2, i, n:n + 1],
                                                 in1=x[:, i, t0:t0 + t], op0=ALU.mult, op1=ALU.add).then_inc(tile_free[g % 2], 2 // len(pp))
                make_gains(l, 1)
                make_gate(l, 1)
                norm(2 * l + 1)

                def up(i):
                    for j in range(4):
                        split_lo(W_UP[l] + j + AHEAD, i, 4)
                        g = G_UP[l] + j
                        freed(dve, g, 4 * i)
                        if l > 0 or j >= 2 or not isinstance(i, int):
                            dve.wait_ge(hid_ready, l * N_UP - 1 + j + 4 * i)
                        dve.tensor_tensor(hid32[:, j % 2, 0:T], relu[:, g % 2, 0:T], relu[:, g % 2, 0:T], ALU.mult).then_inc(hid32_ready, 1)
                        if l == 0 and j == 0 and not (isinstance(i, int) and i == 0):
                            ada_mod(1, -1, i)

                def down(i, last=False):
                    for j in range(8):
                        if not (last and j >= 8 - AHEAD):
                            split_lo(W_DOWN[l] + j + AHEAD, i, 8)
                        if j % 4 == 3:
                            g = G_DOWN[l] + j // 4
                            dve.wait_ge(unit_used, W_DOWN[l] + j + 1 + 8 * i)
                            for n, (t0, t) in enumerate(pp):
                                xs = x[:, bass.ds(2 * i + j // 4, 1), t0:t0 + t]
                                dve.scalar_tensor_tensor(out=xs, in0=bank(g % 2 + 2 * n, t).unsqueeze(1),
                                                         scalar=gains[:, 5, bass.ds(2 * i + j // 4, 1), n], in1=xs,
                                                         op0=ALU.mult, op1=ALU.add).then_inc(tile_free[g % 2], 2 // len(pp))
                        if l == 0 and j == 0:
                            ada_mod(1, N_UP // 4 - 1, i)

                up(0)
                with dve.Fori(1, N_UP // 4) as i:
                    up(i)
                down(0)
                with dve.Fori(1, N_DOWN // 8 - 1) as i:
                    down(i)
                down(N_DOWN // 8 - 1, l == DEPTH - 1)
                if l == 0:
                    ada_mod(1, ADA_BLOCKS - 1)
            norm(NORMS - 1)

        @block.gpsimd
        def _(pool):
            links = [0]

            def link(ins):
                links[0] += 1
                ins.then_inc(pool_chain, 1)
                pool.wait_ge(pool_chain, links[0])

            def add_squares(idx):
                T = norm_tokens(idx)
                link(pool.memset(sq_sum[:, 0:T], 0.0))
                for k in range(KC):
                    pool.wait_ge(sq_ready, KC * idx + k + 1)
                    if k > 0:
                        pool.wait_ge(sq_added, KC * idx + k)
                    pool.tensor_tensor(sq_sum[:, 0:T], sq_sum[:, 0:T], sq[:, k % 2, 0:T], ALU.add).then_inc(sq_added, 1)

            def norm(idx):
                T = norm_tokens(idx)
                for k in range(KC):
                    pool.wait_ge(hhi_ready, KC * idx + k + 1)
                    pool.tensor_tensor(act_lo[:, k, 0:T], h32[:, k, 0:T], act_hi[:, k, 0:T], ALU.subtract).then_inc(act_ready, 1)

            pool.wait_ge(small_here, 16)
            for l in range(DEPTH):
                s = S[l]
                T = tokens(l)
                pp = parts(T)
                if l == 0:
                    add_squares(0)
                norm(2 * l)
                pool.wait_ge(act_ready, KC * (2 * l + 1))
                for c in range(2):
                    for t in (0, 8 + LAT, PADW - 8):
                        link(pool.memset(pa[:, c, t:t + 8], 0.0))
                link(pool.memset(kpad[HD:P, 0, :], 0.0))
                link(pool.memset(kpad[0:HD, 1, :], 0.0))
                link(pool.memset(cum_b[:, 0, :, 0:1], 0.0))
                pool.memset(cum_b[:, 1, :, 0:1], 0.0).then_inc(s["zeroed"], 1)
                for c in range(2):
                    freed(pool, G_IN[l] + c)
                    u, a, b = pa[:, c, :], pool_a, pool_b
                    link(pool.tensor_tensor(a[:, 1:PADW], u[:, 0:PADW - 1], u[:, 1:PADW], ALU.add))
                    if c == 1:
                        link(pool.tensor_tensor(b[:, 2:PADW - 1], a[:, 1:PADW - 2], a[:, 3:PADW], ALU.add))
                        link(pool.tensor_tensor(a[:, 4:PADW - 3], b[:, 2:PADW - 5], b[:, 6:PADW - 1], ALU.add))
                        far = 4
                    else:
                        far = 1
                    hi_rows = slice(HD, P)
                    link(pool.tensor_tensor(b[hi_rows, 8:PADW - 8], a[hi_rows, 8 - far:PADW - 8 - far], a[hi_rows, 8 + far:PADW - 8 + far], ALU.add))
                    for r, buf in ((slice(0, HD), a), (hi_rows, b)):
                        for ei, t in enumerate(EDGES):
                            at = SMALL["edge"][0] + 32 * c + 8 * ei
                            link(pool.tensor_tensor(buf[r, t:t + 8], buf[r, t:t + 8], small[r, at:at + 8], ALU.mult))
                        iw = SMALL["inv_window"][0] + c
                        link(pool.tensor_scalar(buf[r, 8:PADW - 8], buf[r, 8:PADW - 8], small[r, iw:iw + 1], 1.0, ALU.mult, ALU.mult))
                        ins = pool.tensor_tensor(pa[r, c, 8:PADW - 8], buf[r, 8:PADW - 8], pa[r, c, 8:PADW - 8], ALU.subtract)
                        if r.start == 0:
                            link(ins)
                        else:
                            ins.then_inc(s["pool_diff"], 1)
                            pool.wait_ge(s["pool_diff"], c + 1)
                for c in range(2):
                    pool.wait_ge(s["pool_hi"], c + 1)
                    pool.tensor_tensor(act_lo[:, c, 0:T], pa[:, c, 0:T], act_hi[:, c, 0:T], ALU.subtract).then_inc(s["pool_lo"], 1)
                pool.wait_ge(s["pool_lo"], 2)
                pool.memset(state[:, :, :, :], 0.0).then_inc(s["state_zero"], 1)
                quads = quads_of(l < DEPTH - 1)
                for qn, (n, j, keys, nl) in enumerate(quads):
                    pool.wait_ge(s["rinv"], qn + 1)
                    for c in (0, 1):
                        v = prob[:, qn % 2, c, 0:P * len(keys)]
                        pool.tensor_scalar(v, v, stat[:, qn % 2, 5, c:c + 1], A_SCALE, ALU.mult, ALU.mult).then_inc(s["normed"], 1)
                pool.wait_ge(s["pv_done"], sum(len(q[2]) for q in quads))
                for _, _, _, _, q in levels:
                    link(pool.memset(q[HD:P, 0, :], 0.0))
                    link(pool.memset(q[0:HD, 1, :], 0.0))
                for c in range(2):
                    for v in range(LEVELS):
                        h = P >> (v + 1)
                        m = c * LEVELS + v
                        diff = levels[(v + 1) % 2][0]
                        if v == 1:
                            pool.wait_ge(s["w_inter"], 4 * (c + 1))
                        elif m > 0:
                            pool.wait_ge(s["e_ready"], 4 * (m - (v > 0)))
                        nb = T // (2 * h)
                        f = cum_f[:, c, 0:T // P, :].rearrange("p b (n t) -> p (b n) t", t=2 * h)
                        pool.tensor_tensor(diff[:, 0, 0:T].rearrange("p (n t) -> p n t", t=2 * h), f, f[:, :, h - 1:h].broadcast_to([P, nb, 2 * h]),
                                           ALU.subtract).then_inc(s["d_ready"], 1)
                        for b in range(T // P):
                            g_ = cum_b[:, c, b, 0:P].rearrange("p (n t) -> p n t", t=2 * h)
                            ins = pool.tensor_tensor(diff[:, 1, b * P:(b + 1) * P].rearrange("p (n t) -> p n t", t=2 * h), g_,
                                                     g_[:, :, h:h + 1].broadcast_to([P, P // (2 * h), 2 * h]), ALU.subtract)
                            if b < T // P - 1:
                                links[0] += 1
                                ins.then_inc(pool_chain, 1)
                        ins.then_inc(s["d_ready"], 1)
                pool.wait_ge(s["o_done"], 2)
                add_squares(2 * l + 1)
                norm(2 * l + 1)

                def up(i):
                    for j in range(4):
                        u = 4 * i + j
                        pool.wait_ge(hidhi_ready, l * N_UP + 1 + j + 4 * i)
                        pool.tensor_tensor(hid[:, 1, bass.ds(u, 1), 0:T], hid32[:, j % 2, 0:T].unsqueeze(1), hid[:, 0, bass.ds(u, 1), 0:T],
                                           ALU.subtract).then_inc(hid_ready, 1)

                with pool.Fori(0, N_UP // 4) as i:
                    up(i)
                pool.wait_ge(hid_ready, (l + 1) * N_UP)
                add_squares(2 * l + 2)

        @block.tensor
        def _(pe):
            def product(w, g, T, moving, k0, start, stop, i=0, per_w=0, per_n=0, per_g=0):
                n, more = place(W_AT, w, i, per_w, per_n)
                pe.wait_ge(stage_taken[n % RING], n // RING + 1 + more * i)
                if start and g >= 2:
                    pe.wait_ge(tile_free[g % 2], 2 * (g // 2) + per_g * i)
                hi, lo = moving
                for k in range(KC):
                    wh, wl = (b[:, w % RING, k * P:(k + 1) * P] for b in (w_hi, w_lo))
                    for which, (wt, m) in enumerate(((wh, hi), (wh, lo), (wl, hi))):
                        for b, (t0, t) in enumerate(parts(T)):
                            mm = pe.matmul(bank(g % 2 + 2 * b, t), wt, m[:, k0 + k, t0:t0 + t], start=(start and k == 0 and which == 0),
                                           stop=(stop and k == KC - 1 and which == 2), skip_group_check=True)
                mm.then_inc(unit_used, 1)

            def first_products(w, g, T, norms):
                for u in range(2):
                    n = W_AT[w + u]
                    pe.wait_ge(stage_taken[n % RING], n // RING + 1)
                    if g >= 2:
                        pe.wait_ge(tile_free[(g + u) % 2], 2 * ((g + u) // 2))
                for k in range(KC):
                    pe.wait_ge(act_ready, KC * norms + k + 1)
                    for u in range(2):
                        wh, wl = (b[:, (w + u) % RING, k * P:(k + 1) * P] for b in (w_hi, w_lo))
                        for which, (wt, m) in enumerate(((wh, act_hi), (wh, act_lo), (wl, act_hi))):
                            for b, (t0, t) in enumerate(parts(T)):
                                mm = pe.matmul(bank((g + u) % 2 + 2 * b, t), wt, m[:, k, t0:t0 + t], start=(k == 0 and which == 0),
                                               stop=(k == KC - 1 and which == 2), skip_group_check=True)
                        if k == KC - 1:
                            mm.then_inc(unit_used, 1)

            def product_tokens(w, g):
                n = W_AT[w]
                pe.wait_ge(stage_taken[n % RING], n // RING + 1)
                pe.wait_ge(tile_free[g % 2], 2 * (g // 2))
                for b in range(NB):
                    dst = bank(g % 2 + 2 * (b >= LB), P, P * (b % LB))
                    for k in range(KC):
                        wh, wl = (q[:, w % RING, k * P:(k + 1) * P] for q in (w_hi, w_lo))
                        ah, al = (q[:, k, b * P:(b + 1) * P] for q in (act_hi, act_lo))
                        for which, (st, mv) in enumerate(((ah, wh), (ah, wl), (al, wh))):
                            mm = pe.matmul(dst, st, mv, start=(k == 0 and which == 0), stop=(k == KC - 1 and which == 2), skip_group_check=True)
                mm.then_inc(unit_used, 1)

            def ada_unit(a, i=0, per_n=0, per_a=0):
                n, more = place(A_AT, a, i, per_a, per_n)
                pe.wait_ge(stage_full[n % RING], 16 * (n // RING + 1) + 16 * more * i)
                if a % 4 == 0 and a // 4 > 0:
                    pe.wait_ge(ada_copied, a // 4 + (per_a // 4) * i)
                q, kh = a % 4 // 2, a % 2
                for e in range(4):
                    mm = pe.matmul(bank(6, 256, 256 * q)[32 * e:32 * e + 32, :], silu_c[:, 4 * kh + e, :], stage[:, n % RING, 256 * e:256 * e + 256],
                                   start=(kh == 0), stop=(kh == 1), skip_group_check=True)
                mm.then_inc(stage_taken[n % RING], 1)

            def ada_tile(b):
                for a in range(4 * b, 4 * b + 4):
                    ada_unit(a)

            def ada_transpose(b, i=0):
                pe.wait_ge(ada_copied, b + 1 + i)
                if b > 0:
                    pe.wait_ge(mod_ready, b + i)
                for q in range(4):
                    mm = pe.matmul(bank(7, 2, 2 * q), ada_row[:, q * P:(q + 1) * P], sm("sel"), start=True, stop=True, skip_group_check=True)
                mm.then_inc(ada_cols, 1)

            def norm(idx):
                T = norm_tokens(idx)
                pe.wait_ge(sq_added, KC * (idx + 1))
                for b, (t0, t) in enumerate(parts(T)):
                    mm = pe.matmul(bank(4 + b, t), ones, sq_sum[:, t0:t0 + t], start=True, stop=True, skip_group_check=True)
                mm.then_inc(sq_used, 1)

            def value_product(s, m, n, j, keys, ki):
                pe.wait_ge(s["pt_copied"], m + 1)
                mm = pe.matmul(bank(6 + n % 2)[HD * j:HD * j + HD, :], va[:, keys[ki], HD * j:HD * j + HD], prob_t[:, m % 2, :],
                               start=(ki == 0), stop=(ki == len(keys) - 1), skip_group_check=True)
                mm.then_inc(s["pv_done"], 1)

            act = (act_hi, act_lo)
            hidden = (hid[:, 0], hid[:, 1])
            pe.wait_ge(setup_done, 1)
            for b in range(4):
                ada_tile(b)
                if b == 2:
                    norm(0)
                ada_transpose(b)
            for l in range(DEPTH):
                s = S[l]
                T = tokens(l)
                pp = parts(T)
                if l > 0:
                    norm(2 * l)
                for i, (name, c) in enumerate(IN_ORDER):
                    w, g = W_IN[l] + i, G_IN[l] + i
                    if i == 0:
                        first_products(w, g, in_tokens(l, name), 2 * l)
                    elif i == 1:
                        pass
                    elif name in TOKEN_MAJOR:
                        product_tokens(w, g)
                    else:
                        product(w, g, in_tokens(l, name), act, 0, True, True)
                    if l == 0 and i % 2 == 0 and i > 0:
                        ada_transpose(3 + i // 2)
                    if l == 0 and i < 16:
                        ada_unit(16 + 2 * i)
                        ada_unit(17 + 2 * i)
                freed(pe, G_IN[l] + N_IN - 2)
                freed(pe, G_IN[l] + N_IN - 1)
                pe.wait_ge(masks_ready, 2)
                for c in range(2):
                    pe.wait_ge(s["pool_diff"], c + 1)
                    for b, (t0, t) in enumerate(pp):
                        mm = pe.matmul(bank(2 * c + b, t), sm("pool_w", (2 * l + c) * P, P), pa[:, c, SEG[b][0]:SEG[b][0] + t], start=True, stop=True,
                                       skip_group_check=True)
                    mm.then_inc(s["pool_mm"], 1)

                quads = quads_of(l < DEPTH - 1)
                pe.wait_ge(s["roped"], 6)
                pe.wait_ge(s["pool_y"], 2 * len(pp))
                if l == 0:
                    pe.wait_ge(mod_ready, ADA_BLOCKS)
                pt = 0
                waiting = []
                for scored, turned in attention_steps(quads):
                    if scored:
                        qn, c = scored
                        n, j, keys, nl = quads[qn]
                        it = 4 * qn + c
                        if it >= 2:
                            pe.wait_ge(s["exped"], it - 1)
                        q = qa[:, c, n * P:n * P + P]
                        b = 2 * (it % 2)
                        if nl:
                            at = 512 - P * nl
                            pe.matmul(bank(b, P * nl, at), q, kpad[:, j, keys[0] * P:keys[0] * P + P * nl], start=True, stop=False, skip_group_check=True)
                            masked = [(kb, m) for kb, m in ((n - 1, 0), (n + 1, 1)) if kb in keys[:nl]]
                            for kb, m in masked:
                                pe.matmul(bank(b, P, at + P * keys.index(kb)), band[:, 0:P], band[:, (1 + m) * P:(2 + m) * P],
                                          start=False, stop=(kb, m) == masked[-1], skip_group_check=True)
                        pe.matmul(bank(b + 1, CTX), q, kpad[:, j, LAT:TOK], start=True, stop=True, skip_group_check=True).then_inc(s["scores"], 1)
                    for m, qn, ki in waiting:
                        n, j, keys, nl = quads[qn]
                        if ki == 0 and j == 0 and qn >= 4:
                            pe.wait_ge(s["o_lo"], qn // 2 - 1)
                        value_product(s, m, n, j, keys, ki)
                    waiting = []
                    for qn, ki in turned:
                        if ki == 0:
                            pe.wait_ge(s["normed"], 2 * (qn + 1))
                            pe.wait_ge(s["normed_v"], 2 * (qn + 1))
                        if pt >= 2:
                            pe.wait_ge(s["pt_copied"], pt - 1)
                        for c in range(4):
                            mm = pe.transpose(bank(4 + pt % 2, P, P * c), prob[:, qn % 2, c, P * ki:P * ki + P], ident)
                        mm.then_inc(s["pt_done"], 1)
                        waiting.append((pt, qn, ki))
                        pt += 1

                nsp = T // P
                pe.wait_ge(s["o_lo"], len(quads) // 2)
                for c in range(2):
                    if c == 1:
                        pe.wait_ge(s["oy"], 1)
                        pe.wait_ge(s["a_copied"], LEVELS + 1)
                    for d, src in enumerate((ek, eq)):
                        pe.wait_ge(s["w_inter"], 4 * c + d + 1)
                        for b in range(NB):
                            mm = pe.transpose(ps[:, 1024 * d + b * P:1024 * d + b * P + P], src[:, b * P:b * P + P], ident)
                        mm.then_inc(s["kt_tr"], 1)
                    for d, order in enumerate((F_ORDER, B_ORDER)):
                        pe.wait_ge(s["kt_copied"], 2 * c + d + 1)
                        for m in range(NB - 1):
                            b = order[m]
                            at = (4 + 2 * d) * 512 + P * m
                            mm = pe.matmul(ps[:, at:at + P], kt[:, d, b, :], hv[:, c, b, :], start=True, stop=True, skip_group_check=True)
                    mm.then_inc(s["p_done"], 1)
                    for v in range(LEVELS + 1):
                        m = c * (LEVELS + 1) + v
                        pe.wait_ge(s["m_ready"], 4 * (m + 1))
                        if v == 1:
                            pe.wait_ge(s["st_ready"], 10 * (c + 1))
                        if v >= 2:
                            pe.wait_ge(s["a_copied"], m - 1)
                        km_v, qm_v = levels[(v + 1) % 2][3:]
                        for b in range(nsp):
                            mm = pe.matmul(bank(3 * (v % 2) + b // 2, 2 * P, 2 * P * (b % 2)), km_v[:, b * P:b * P + P], qm_v[:, :, b * P:b * P + P],
                                           start=True, stop=True, skip_group_check=True)
                        mm.then_inc(s["a_done"], 1)
                    pe.wait_ge(s["st_ready"], 10 * (c + 1))
                    pe.wait_ge(s["a_copied"], (LEVELS + 1) * (c + 1))
                    for b in range(nsp):
                        dst = bank(6 + (b >= LB), P, P * (b % LB))
                        for h in range(2):
                            r = slice(HD * h, HD * h + HD)
                            pe.matmul(dst[r, :], hv[:, c, b, r], amat[:, b, h, :], start=True, stop=False, skip_group_check=True)
                        come = [d for d, order in enumerate((F_ORDER, B_ORDER)) if b != order[0]]
                        for d in come:
                            mm = pe.matmul(dst, state[:, d, b, :], qi[:, d, b * P:b * P + P], start=False, stop=d == come[-1], skip_group_check=True)
                    mm.then_inc(s["o_done"], 1)
                    pe.wait_ge(s["osq"], (c + 1) * len(pp))
                    for b, (t0, t) in enumerate(pp):
                        mm = pe.matmul(bank(b, t), pair_ones, ek[:, t0:t0 + t], start=True, stop=True, skip_group_check=True)
                    mm.then_inc(s["oss"], 1)

                pe.wait_ge(s["pool_lo"], 2)
                pe.wait_ge(s["oy_lo"], 2)
                for i in range(N_OUT):
                    product(W_OUT[l] + i, G_OUT[l] + i, T, act, 0, True, True)
                norm(2 * l + 1)

                def up(i):
                    for j in range(4):
                        if isinstance(i, int) and j < 2:
                            if j == 0:
                                first_products(W_UP[l], G_UP[l], T, 2 * l + 1)
                        else:
                            product(W_UP[l] + j, G_UP[l] + j, T, act, 0, True, True, i, 4, 8 if l == 0 else 4, 4)
                        if l == 0:
                            if j == 0 and not (isinstance(i, int) and i == 0):
                                ada_transpose(ADA_BLOCKS - 1, i)
                            ada_unit(4 * ADA_BLOCKS + j, i, 8, 4)

                def down(i):
                    for j in range(8):
                        product(W_DOWN[l] + j, G_DOWN[l] + j // 4, T, hidden, KC * (j % 4), j % 4 == 0, j % 4 == 3, i, 8, 12 if l == 0 else 8, 2)
                        if l == 0 and j == 0:
                            ada_transpose(ADA_BLOCKS + N_UP // 4 - 1, i)
                        if l == 0 and j % 2 == 0:
                            ada_unit(4 * ADA_BLOCKS + N_UP + j // 2, i, 12, 4)

                up(0)
                with pe.Fori(1, N_UP // 4) as i:
                    up(i)
                pe.wait_ge(hid_ready, (l + 1) * N_UP)
                down(0)
                with pe.Fori(1, N_DOWN // 8) as i:
                    down(i)
                if l == 0:
                    ada_transpose(2 * ADA_BLOCKS - 1)
            norm(NORMS - 1)


def _constants():
    p = np.arange(P)
    out = {"sel": np.zeros((P, 2)), "inv_window": np.zeros((P, 2)), "edge": np.zeros((P, 2, 4, 8))}
    out["sel"][np.arange(4) * 32, 0] = 1
    out["sel"][np.arange(4) * 32 + 1, 1] = 1
    for c in range(2):
        for half in range(2):
            w = POOL_WINDOWS[2 * c + half]
            rows = slice(HD * half, HD * half + HD)
            out["inv_window"][rows, c] = 1 / w
            for e, (n, t0) in enumerate(((LAT, 0), (LAT, LAT - 8), (CTX, 0), (CTX, CTX - 8))):
                t = t0 + np.arange(8)
                out["edge"][rows, c, e] = w / (np.minimum(t + w // 2, n) - np.maximum(t - w // 2, 0))
    out["ident"] = np.eye(P)
    out["ones"] = np.ones((P, P))
    out["pair_ones"] = (p[:, None] // HD == p[None, :] // HD)
    t = np.arange(LAT)
    inv = (10000.0 ** (-np.arange(0, HD // 2, 2, dtype=np.float32) / (HD // 2))).astype(np.float32)
    r = p % HD
    place = np.where(r[:, None] < HD // 2, (t // GRID_W)[None, :], (t % GRID_W)[None, :]).astype(np.float32)
    angle = (place * inv[r % 16][:, None]).astype(np.float32)
    out["rope_cos"] = np.cos(angle)
    out["rope_sin"] = np.sin(angle) * np.where(r % 32 < 16, -1, 1)[:, None]
    levels = np.zeros((P, 8, P))
    for v in range(LEVELS):
        h = P >> (v + 1)
        levels[:, v] = (p[:, None] // (2 * h) == p[None, :] // (2 * h)) & (p[:, None] // h != p[None, :] // h)
    levels[:, LEVELS] = np.eye(P)
    band = np.zeros((P, 3, P), np.float32)
    band[:, 0] = np.eye(P)
    band[:, 1] = np.where(p[None, :] < p[:, None], -1e30, 0)
    band[:, 2] = np.where(p[None, :] > p[:, None], -1e30, 0)
    return out, np.concatenate([levels.reshape(P, -1), band.reshape(P, -1)], 1).astype(np.float32)


def _rows(w):
    return w.reshape(-1, P, w.shape[1]).transpose(1, 0, 2)


def _layout(i):
    i = {k: np.ascontiguousarray(v) for k, v in i.items()}
    starts = {"pool": 0, "q": 256, "k": 768, "va": 896, "qh": 1024, "ff": 1280, "fb": 1536, "ih": 1792, "gh": 2048}
    pair = lambda at, c: np.concatenate([at + HD * c + np.arange(HD), at + HD * (4 + c) + np.arange(HD)])
    out_rows = np.concatenate([np.arange(256)] + [pair(256, c) for c in range(4)] + [np.arange(768, D)])
    weights, ada = [], []
    for l in range(DEPTH):
        w_in, w_out = _rows(i["w_in"][l]), _rows(i["w_out"][l][out_rows])
        up, down, wa = _rows(i["w_mlp1"][l]), _rows(i["w_mlp2"][l]), _rows(i["w_ada"][l])
        for name, c in IN_ORDER:
            cols = pair(starts[name], c) if name == "q" else starts[name] + P * c + np.arange(P)
            weights.append(w_in[:, :, cols])
        weights += [w_out[:, :, k * P:k * P + P] for k in range(KC)]
        weights += [up[:, :, k * P:k * P + P] for k in range(FU)]
        weights += [down[:, KC * q:KC * q + KC, k * P:k * P + P] for k in range(KC) for q in range(4)]
        ada += [wa[:, 4 * kh:4 * kh + 4, b * 512 + 256 * q:b * 512 + 256 * q + 256]
                for b in range(ADA_BLOCKS) for q in range(2) for kh in range(2)]
    stream = np.empty((len(STREAM), P, UNIT), np.float32)
    for n, (kind, u) in enumerate(STREAM):
        stream[n] = (weights if kind == "w" else ada)[u].reshape(P, UNIT)
    small = np.zeros((P, N_SMALL), np.float32)

    def put(name, a):
        at, n = SMALL[name]
        small[:, at:at + n] = np.asarray(a, np.float32).reshape(P, n)

    cols = lambda v: np.moveaxis(v.reshape(v.shape[:-1] + (-1, P)), -1, 0)
    put("c", np.stack([cols(i["c"][0]), cols(i["c_ctx"])], -1))
    put("b_ada", cols(i["b_ada"]))
    for name, key in (("norm1", "norm1_w"), ("norm2", "norm2_w"), ("final", "final_norm_w"), ("pool_scale", "pool_scale"), ("lower", "hg_lower")):
        put(name, cols(i[key]))
    put("hg_norm", np.tile(i["hg_norm_w"].T, (2, 1)))
    put("sink", np.tile(i["attn_sink"].reshape(1, -1), (P, 1)))
    blocks = np.zeros((P, DEPTH, 2, P), np.float32)
    for l in range(DEPTH):
        for g in range(4):
            r = slice(HD * (g % 2), HD * (g % 2) + HD)
            blocks[r, l, g // 2, r] = i["pool_w"][l, g]
    put("pool_w", blocks)
    constants, masks = _constants()
    for name, a in constants.items():
        put(name, a)
    xin = np.ascontiguousarray(np.concatenate([i["x"][0], i["ctx"][0]], 0).T)
    return {"stream": stream, "xin": xin, "small": small, "masks": masks}


def kernel(**inputs):
    import concourse.bacc as bacc
    from concourse.bass_utils import run_bass_kernel_spmd

    arrays = _layout({k: np.asarray(v) for k, v in inputs.items()})
    nc = bacc.Bacc("TRN2", target_bir_lowering=False, num_devices=1)
    args = [nc.dram_tensor(f"in_{k}", a.shape, mybir.dt.from_np(a.dtype), kind="ExternalInput").ap() for k, a in arrays.items()]
    out = nc.dram_tensor("result", (D, LAT), F32, kind="ExternalOutput").ap()
    build_program(nc, *args, out)
    r = run_bass_kernel_spmd(nc, [{f"in_{k}": a for k, a in arrays.items()}], core_ids=[0])
    return np.asarray(r.results[0]["result"]).T[None]
```

```python
from contextlib import ExitStack

import numpy as np
import concourse.bass as bass
from concourse import mybir

F32, F16, BF16, U8 = mybir.dt.float32, mybir.dt.float16, mybir.dt.bfloat16, mybir.dt.uint8
ALU = mybir.AluOpType
ACT = mybir.ActivationFunctionType
AX_X = mybir.AxisListType.X

P = 128
D = 1024
KC = D // P
LAT, CTX = 512, 256
TOK = LAT + CTX
NB = TOK // P
LB = LAT // P
DEPTH = 2
HD = 64
QH, KVH = 8, 2
FF = 4 * D
FU = FF // P
EPS = 1e-6
GRID_W = 64
POOL_WINDOWS = (2, 4, 8, 16)

W_SCALE = 256.0
A_SCALE = 64.0
H_SCALE = 1.0
UNSCALE = 1.0 / (W_SCALE * A_SCALE)
UNSCALE2 = 1.0 / (W_SCALE * H_SCALE)

RING = 4
AHEAD = 2
UNIT = KC * P
N_IN, N_OUT, N_UP, N_DOWN = 18, KC, FU, KC * (FF // D)
ADA_BLOCKS = 6 * D // 512
IN_ORDER = [("pool", 0), ("pool", 1), ("ff", 0), ("ff", 1), ("fb", 0), ("fb", 1), ("qh", 0), ("qh", 1),
            ("ih", 0), ("ih", 1), ("k", 0), ("q", 0), ("q", 1), ("q", 2), ("q", 3), ("gh", 0), ("gh", 1), ("va", 0)]
TOKEN_MAJOR = ("ih", "va")
LOGS_AT = 8
SUMS_AT = 9
KEYS_STEP, QUERIES_STEP = -6, -2
CTX_NEEDED_LAST = ("ff", "fb", "ih", "k", "va")


def plan_stream():
    out, w, a = [], 0, 0

    def weight():
        nonlocal w
        if w < DEPTH * (N_IN + N_OUT + N_UP + N_DOWN):
            out.append(("w", w))
            w += 1

    def ada(n):
        nonlocal a
        out.extend(("a", a + i) for i in range(n))
        a += n

    ada(16)
    for _ in range(AHEAD):
        weight()
    for l in range(DEPTH):
        for i in range(N_IN):
            weight()
            if l == 0 and i < 16:
                ada(2)
        for _ in range(N_OUT):
            weight()
        for _ in range(N_UP):
            weight()
            if l == 0:
                ada(1)
        for i in range(N_DOWN):
            weight()
            if l == 0 and i % 2 == 0:
                ada(1)
    return out


STREAM = plan_stream()
W_AT = {i: n for n, (kind, i) in enumerate(STREAM) if kind == "w"}
A_AT = {i: n for n, (kind, i) in enumerate(STREAM) if kind == "a"}
N_WEIGHTS = len(W_AT)
assert len(STREAM) % RING == 0


def place(where, u, i, per_u, per_n):
    if isinstance(i, int):
        return where[u + per_u * i], 0
    return where[u + per_u] - per_n, per_n // RING

SMALL = {}
_at = 0
for _name, _n in [("c", 2 * KC), ("b_ada", DEPTH * 48), ("norm1", DEPTH * KC), ("norm2", DEPTH * KC), ("final", KC),
                  ("pool_scale", DEPTH * 2), ("lower", DEPTH * 4), ("hg_norm", DEPTH), ("sink", DEPTH * QH),
                  ("sel", 2), ("inv_window", 2), ("edge", 2 * 32), ("ident", P), ("ones", P), ("pair_ones", P),
                  ("rope_cos", LAT), ("rope_sin", LAT), ("pool_w", DEPTH * 2 * P)]:
    SMALL[_name] = (_at, _n)
    _at += _n
N_SMALL = _at

SEG = ((8, 0, LAT), (8 + LAT + 8, LAT, CTX))
PADW = 8 + LAT + 8 + CTX + 8
EDGES = (8, LAT, 8 + LAT + 8, LAT + 8 + CTX)
LEVELS = 7
F_ORDER = (4, 5, 0, 1, 2, 3)
B_ORDER = (5, 4, 3, 2, 1, 0)
SWAP = [(r + 16) % 32 for r in range(32)]


def quads_of(ctx):
    out = []
    for n in range(LB):
        local = [b for b in (n - 1, n, n + 1) if 0 <= b < LB]
        out += [(n, j, local + [4, 5], len(local)) for j in range(KVH)]
    if ctx:
        out += [(n, j, [4, 5], 0) for n in (4, 5) for j in range(KVH)]
    return out


def attention_steps(quads):
    steps = []
    for n in range(4 * len(quads) + 8):
        qn, c = divmod(n, 4)
        q, blocks = (qn - 1, [c - 1]) if c else (qn - 2, [3, 4])
        steps.append(((qn, c) if qn < len(quads) else None,
                      [(q, k) for k in blocks if 0 <= q < len(quads) and k < len(quads[q][2])]))
    return steps


def outputs_of(quads):
    steps, done, out = attention_steps(quads), 0, {}
    for n, (_, turned) in enumerate(steps):
        for q, k in turned:
            done += 1
            if q % 2 == 1 and k == len(quads[q][2]) - 1:
                out[n + 2] = (q // 2, quads[q][0], done)
    return out


def build_program(nc, stream, xin, small_in, masks_in, out):
    stack = ExitStack()
    with stack:
        def sb(name, shape, dt=F32):
            return stack.enter_context(nc.sbuf_tensor(name, shape, dt))

        def sem(name):
            return stack.enter_context(nc.semaphore(name))

        x = sb("x", [P, KC, TOK])
        act_hi = sb("act_hi", [P, KC, TOK], F16)
        act_lo = sb("act_lo", [P, KC, TOK], F16)
        arena = sb("arena", [P, FU * TOK + 64])
        stage = sb("stage", [P, RING, UNIT])
        w_hi = sb("w_hi", [P, RING, UNIT], F16)
        w_lo = sb("w_lo", [P, RING, UNIT], F16)
        small = sb("small", [P, N_SMALL])
        masks = sb("masks", [P, 8, HD], U8)
        zeros = sb("zeros", [P, P], BF16)
        band = sb("band", [P, 3 * P], BF16)
        extra = sb("extra", [P, 4 * TOK])
        ada_row = sb("ada_row", [P, 512])
        rst = sb("rst", [P, TOK])
        mod = [sb(f"mod{l}", [P, 48, 2]) for l in range(DEPTH)]
        gains = sb("gains", [P, 6, KC, 2])
        silu_c = sb("silu_c", [P, KC, 32])
        sig_c = sb("sig_c", [P, KC, 2])
        nw64 = sb("nw64", [P, DEPTH * 2 * KC])
        lbt = sb("lbt", [P, DEPTH, 2, 4])
        lwork = sb("lwork", [P, 3, 4])
        hgw = sb("hgw", [P, DEPTH])
        psc = sb("psc", [P, DEPTH * 2])
        eps_t = sb("eps_t", [P, 1])
        neg_sink = sb("neg_sink", [P, DEPTH * QH])
        stat = sb("stat", [P, 2, 6, 4])
        dec = sb("dec", [P, 2, NB])

        def sm(name, i=0, n=None):
            at, size = SMALL[name]
            return small[:, at + i:at + (size if n is None else i + n)]

        ident, ones, pair_ones = sm("ident"), sm("ones"), sm("pair_ones")
        hid = arena[:, 0:FU * TOK].bitcast(F16).rearrange("p (h u t) -> p h u t", h=2, u=FU)
        h32 = arena[:, 0:KC * TOK].rearrange("p (k t) -> p k t", k=KC)

        masks32 = arena[:, 0:7 * P]

        def cutter(tensor, at, end):
            pos = [at]

            def take(n):
                assert pos[0] + n <= end, (pos[0], n, end)
                pos[0] += n
                return tensor[:, pos[0] - n:pos[0]]
            return take, pos

        take, pos = cutter(arena, 0, FU * TOK + 64)
        pa = take(2 * PADW).rearrange("p (c t) -> p c t", c=2)
        qa = take(4 * TOK).rearrange("p (c t) -> p c t", c=4)
        kpad = take(2 * TOK).rearrange("p (j t) -> p j t", j=2)
        va = take(TOK).rearrange("p (b v) -> p b v", b=NB)
        hv = take(2 * TOK).rearrange("p (c b v) -> p c b v", c=2, b=NB)
        qs = take(2 * TOK).rearrange("p (c t) -> p c t", c=2)
        kk = take(4 * TOK).rearrange("p (d c t) -> p d c t", d=2, c=2)
        cum_f = take(2 * TOK).rearrange("p (c b t) -> p c b t", c=2, b=NB)
        cum_b = take(2 * NB * 129).rearrange("p (c b t) -> p c b t", c=2, b=NB)
        gate = take(2 * TOK).rearrange("p (c t) -> p c t", c=2)
        shared = pos[0]
        gbuf = take(4 * TOK).rearrange("p (g t) -> p g t", g=4)
        sgt = take(2 * TOK).rearrange("p (s t) -> p s t", s=2)
        rot = take(2 * LAT).rearrange("p (s t) -> p s t", s=2)
        pos[0] = shared
        prob = take(8 * 640).rearrange("p (s c k) -> p s c k", s=2, c=4)
        prob_t = take(2 * 512).rearrange("p (s n) -> p s n", s=2)
        pos[0] = shared
        diag = take(2 * TOK).rearrange("p (c b h t) -> p c b h t", c=2, b=NB, h=2)
        amat = [take(2 * TOK).rearrange("p (b h t) -> p b h t", b=NB, h=2)]
        level_at = pos[0]
        levels = []
        for pos[0] in (level_at, 2 * PADW):
            levels.append((take(TOK), take(TOK), take(TOK), take(2 * TOK).rearrange("p (h t) -> p h t", h=2)))
        amat.append(take(2 * TOK).rearrange("p (b h t) -> p b h t", b=NB, h=2))
        kd = arena[:, 0:2 * TOK].rearrange("p (d t) -> p d t", d=2)
        kt = arena[:, 0:2 * TOK].rearrange("p (d b k) -> p d b k", d=2, b=NB)
        take, pos = cutter(extra, 0, 4 * TOK)
        pool_a, pool_b = take(PADW), take(PADW)
        pos[0] = 0
        state = take(2 * NB * P).rearrange("p (d b v) -> p d b v", d=2, b=NB)
        qi = take(2 * TOK).rearrange("p (d t) -> p d t", d=2)
        pos[0] = 0
        relu = take(2 * TOK).rearrange("p (s t) -> p s t", s=2)
        hid32 = take(2 * TOK).rearrange("p (s t) -> p s t", s=2)
        sq = relu
        sq_sum = hid32[:, 1, :]

        ps = stack.enter_context(nc.psum_tensor("ps", [P, 8 * 512], F32))

        def bank(b, n=512, at=0):
            return ps[:, b * 512 + at:b * 512 + at + n]

        stage_full = [sem(f"stage_full{i}") for i in range(RING)]
        stage_taken = [sem(f"stage_taken{i}") for i in range(RING)]
        hi_ready = sem("hi_ready")
        unit_used = sem("unit_used")
        tile_free = [sem("tile_free0"), sem("tile_free1")]
        small_here, x_here, masks_here, masks_ready = sem("small_here"), sem("x_here"), sem("masks_here"), sem("masks_ready")
        setup_v, setup_a, setup_done = sem("setup_v"), sem("setup_a"), sem("setup_done")
        ada_copied, ada_cols, mod_ready = sem("ada_copied"), sem("ada_cols"), sem("mod_ready")
        sq_ready, sq_added, sq_used = sem("sq_ready"), sem("sq_added"), sem("sq_used")
        rst_log, rst_ready = sem("rst_log"), sem("rst_ready")
        h_scaled, h32_ready, hhi_ready, act_ready = sem("h_scaled"), sem("h32_ready"), sem("hhi_ready"), sem("act_ready")
        hid32_ready, hidhi_ready, hid_ready = sem("hid32_ready"), sem("hidhi_ready"), sem("hid_ready")
        out_ready, out_sent = sem("out_ready"), sem("out_sent")
        dve_chain, pool_chain = sem("dve_chain"), sem("pool_chain")
        names = ("pads_zero zeroed rows_zero pool_diff pool_mm pool_y pool_hi pool_lo state_zero sig f_ready k_ready g_ready roped cum_ready "
                 "scores negmax exped esink_in esink rinv normed normed_v pt_done pt_copied pv_done o_hi o_lo "
                 "e_inter w_inter kt_tr kt_copied p_done st_half st_ready s_done d_ready e_ready m_ready a_done off_half off_copied "
                 "diag_copied amat_ready o_done osq og oss orst_log orst oy oy_hi oy_lo").split()
        S = [{n: sem(f"{n}_{l}") for n in names} for l in range(DEPTH)]
        block = stack.enter_context(nc.Block())

        def tokens(l):
            return TOK if l < DEPTH - 1 else LAT

        def parts(t):
            return [(0, LAT)] + ([(LAT, CTX)] if t == TOK else [])

        def in_tokens(l, name):
            return TOK if l < DEPTH - 1 or name in CTX_NEEDED_LAST else LAT

        W_IN = [l * (N_IN + N_OUT + N_UP + N_DOWN) for l in range(DEPTH)]
        W_OUT = [w + N_IN for w in W_IN]
        W_UP = [w + N_OUT for w in W_OUT]
        W_DOWN = [w + N_UP for w in W_UP]
        G_IN = [l * (N_IN + N_OUT + N_UP + KC) for l in range(DEPTH)]
        G_OUT = [g + N_IN for g in G_IN]
        G_UP = [g + N_OUT for g in G_OUT]
        G_DOWN = [g + N_UP for g in G_UP]
        NORMS = 2 * DEPTH + 1

        def freed(eng, g, i=0):
            eng.wait_ge(tile_free[g % 2], 2 * (g // 2 + 1) + i)

        def soon(i):
            return (AHEAD, AHEAD + 1) if i == 0 else () if i == 1 else (i + AHEAD,)

        def taken(eng, s, m):
            c, v = divmod(m, LEVELS + 1)
            if v == 0:
                eng.wait_ge(s["off_copied"], c + 1)
            else:
                eng.wait_ge(s["diag_copied"], LEVELS * c + v)

        def inter_bank(c, d):
            return 2 if (c, d) == (0, 1) else 4

        def own_bank(c, d):
            return 6 if (c, d) == (0, 1) else 4

        def norm_tokens(idx):
            return LAT if idx == NORMS - 1 or idx == 2 * DEPTH - 1 else TOK

        @block.sync
        def _(sp):
            sp.dma_start(small[:, :], small_in).then_inc(small_here, 16)
            for n in range(RING):
                sp.dma_start(stage[:, n, :], stream[n]).then_inc(stage_full[n], 16)
            with sp.Fori(1, len(STREAM) // RING) as i:
                for s in range(RING):
                    sp.wait_ge(stage_taken[s], i)
                    sp.dma_start(stage[:, s, :], stream[RING * i + s]).then_inc(stage_full[s], 16)
            for k in range(KC):
                sp.wait_ge(out_ready, k + 1)
                sp.dma_start(out[k * P:(k + 1) * P, :], h32[:, k, 0:LAT]).then_inc(out_sent, 16)
            sp.wait_ge(out_sent, 16 * KC)

        @block.scalar
        def _(act):
            act.dma_start(x[:, :, :], xin.rearrange("(k p) t -> p k t", p=P)).then_inc(x_here, 16)
            act.dma_start(masks32, masks_in).then_inc(masks_here, 16)

            def split_hi(w, i=0, per_w=0, per_n=0):
                n, more = place(W_AT, w, i, per_w, per_n)
                act.wait_ge(stage_full[n % RING], 16 * (n // RING + 1) + 16 * more * i)
                if w >= RING:
                    act.wait_ge(unit_used, w - RING + 1 + per_w * i)
                act.activation(w_hi[:, w % RING, :], stage[:, n % RING, :], ACT.Copy, scale=W_SCALE).then_inc(hi_ready, 1)

            def ada_copy(b, i=0, per_n=0):
                n, more = place(A_AT, 4 * b + 3, i, 4, per_n)
                act.wait_ge(stage_taken[n % RING], n // RING + 1 + more * i)
                if b > 0:
                    act.wait_ge(ada_cols, b + i)
                act.activation(ada_row[:, :], bank(6), ACT.Copy).then_inc(ada_copied, 1)

            act.wait_ge(small_here, 16)
            act.activation(sig_c[:, :, :], sm("c").rearrange("p (k v) -> p k v", v=2), ACT.Sigmoid).then_inc(setup_a, 1)
            act.wait_ge(setup_v, 1)
            act.activation(lwork[:, 0:2, :], lwork[:, 0:2, :], ACT.Exp).then_inc(setup_a, 1)

            logs = [0]

            def square(idx, k, buf):
                T = norm_tokens(idx)
                if not isinstance(k, int) or k >= 2:
                    act.wait_ge(sq_added, (KC - 1) * idx - 1 + k)
                xs = x[:, k, 0:T] if isinstance(k, int) else x[:, bass.ds(k, 1), 0:T]
                dst = sq[:, buf, 0:T] if isinstance(k, int) else sq[:, buf:buf + 1, 0:T]
                act.activation(dst, xs, ACT.Square).then_inc(sq_ready, 1)

            def inverse_rms(idx):
                act.wait_ge(sq_used, idx + 1)
                T = norm_tokens(idx)
                for n, (t0, t) in enumerate(parts(T)):
                    act.activation(rst[:, t0:t0 + t], bank(4 + n, t), ACT.Ln, bias=eps_t[:, 0:1], scale=1.0 / D).then_inc(rst_log, 1)
                    logs[0] += 1
                act.wait_ge(rst_log, logs[0])
                act.activation(rst[:, 0:T], rst[:, 0:T], ACT.Exp, scale=-0.5).then_inc(rst_ready, 1)

            def split_norm(idx, w):
                split_hi(w)
                T = norm_tokens(idx)
                for k in range(KC):
                    act.wait_ge(h32_ready, idx * KC + k + 1)
                    act.activation(act_hi[:, k, 0:T], h32[:, k, 0:T], ACT.Copy).then_inc(hhi_ready, 1)

            act.wait_ge(setup_done, 1)
            act.wait_ge(x_here, 16)
            for b in range(4):
                for k in range(3 * b, min(3 * b + 3, KC)):
                    square(0, k, k % 2)
                if b == 2:
                    inverse_rms(0)
                ada_copy(b)
            for w in range(AHEAD):
                split_hi(w)

            for l in range(DEPTH):
                s = S[l]
                T = tokens(l)
                pp = parts(T)
                if l > 0:
                    inverse_rms(2 * l)
                split_norm(2 * l, W_IN[l] + AHEAD)

                for i, (name, c) in enumerate(IN_ORDER):
                    g = G_IN[l] + i
                    for w in soon(i)[i == 0:]:
                        split_hi(W_IN[l] + w)
                    if l == 0 and i % 2 == 0 and i > 0:
                        ada_copy(3 + i // 2)
                    pi = parts(in_tokens(l, name))
                    inc = 2 // len(pi)
                    if i == 0:
                        act.wait_ge(s["pads_zero"], 1)
                    if name == "k":
                        act.wait_ge(s["zeroed"], 1)
                    if name == "gh":
                        freed(act, G_IN[l] + IN_ORDER.index(("qh", c)))
                    act.wait_ge(unit_used, W_IN[l] + i + 1)
                    for n, (t0, t) in enumerate(pi):
                        src = bank(g % 2 + 2 * n, t)
                        if name in ("qh", "gh"):
                            act.activation(sgt[:, c, t0:t0 + t], src, ACT.Sigmoid, scale=UNSCALE).then_inc(s["sig"], 1)
                            continue
                        if name == "pool":
                            ins = act.activation(pa[:, c, SEG[n][0]:SEG[n][0] + t], src, ACT.Copy, scale=UNSCALE)
                        elif name in ("ff", "fb"):
                            ins = act.activation(gbuf[:, 2 * (name == "fb") + c, t0:t0 + t], src, ACT.Sigmoid, scale=UNSCALE)
                        elif name == "ih":
                            ins = act.activation(hv[:, c, t0 // P:(t0 + t) // P, :], src.rearrange("p (b v) -> p b v", v=P), ACT.Copy, scale=UNSCALE)
                        elif name == "va":
                            ins = act.activation(va[:, t0 // P:(t0 + t) // P, :], src.rearrange("p (b v) -> p b v", v=P), ACT.Copy, scale=UNSCALE)
                        elif name == "k":
                            for j in range(KVH):
                                h = slice(HD * j, HD * j + HD)
                                ins = act.activation(kpad[h, j, t0:t0 + t], ps[h, (g % 2 + 2 * n) * 512:(g % 2 + 2 * n) * 512 + t], ACT.Copy, scale=UNSCALE)
                        else:
                            ins = act.activation(qa[:, c, t0:t0 + t], src, ACT.Copy, scale=UNSCALE * HD ** -0.5)
                        ins.then_inc(tile_free[g % 2], inc)
                    if i == LOGS_AT:
                        act.wait_ge(s["k_ready"], 4)
                        for gi in range(4):
                            act.activation(gbuf[:, gi, :], gbuf[:, gi, :], ACT.Ln).then_inc(s["g_ready"], 1)
                for c in range(2):
                    act.wait_ge(s["pool_mm"], c + 1)
                    for n, (t0, t) in enumerate(pp):
                        act.activation(pa[:, c, t0:t0 + t], bank(2 * c + n, t), ACT.Copy, scale=psc[:, 2 * l + c:2 * l + c + 1]).then_inc(s["pool_y"], 1)
                    act.wait_ge(s["pool_y"], (c + 1) * len(pp))
                    act.activation(act_hi[:, c, 0:T], pa[:, c, 0:T], ACT.Copy).then_inc(s["pool_hi"], 1)

                nsp = T // P

                def between_keys(c):
                    if c == 0:
                        act.wait_ge(s["state_zero"], 1)
                    else:
                        act.wait_ge(s["p_done"], 2 * c)
                    for b in range(NB):
                        act.activation(kd[:, 0, b * P:b * P + P], cum_f[:, c, b, :], ACT.Exp, bias=cum_f[:, c, b, P - 1:P], scale=-1.0).then_inc(s["e_inter"], 1)
                    act.activation(kd[:, 1, :].rearrange("p (b t) -> p b t", b=NB), cum_b[:, c, :, 0:P], ACT.Exp).then_inc(s["e_inter"], 1)

                def between_queries(c):
                    if c > 0:
                        act.wait_ge(s["s_done"], c)
                    act.activation(qi[:, 0, 0:T].rearrange("p (b t) -> p b t", t=P), cum_f[:, c, 0:nsp, :], ACT.Exp).then_inc(s["e_inter"], 1)
                    for b in range(nsp):
                        act.activation(qi[:, 1, b * P:b * P + P], cum_b[:, c, b, 0:P], ACT.Exp, bias=cum_b[:, c, b, P:P + 1], scale=-1.0).then_inc(s["e_inter"], 1)
                    if c > 0:
                        act.wait_ge(s["st_ready"], 10)
                    act.activation(dec[:, 0, :], cum_f[:, c, :, P - 1], ACT.Exp).then_inc(s["e_inter"], 1)
                    act.activation(dec[:, 1, :], cum_b[:, c, :, P], ACT.Exp).then_inc(s["e_inter"], 1)

                quads = quads_of(l < DEPTH - 1)
                key_blocks = [len(q[2]) for q in quads]
                act.wait_ge(s["cum_ready"], 4)
                freed(act, G_IN[l] + N_IN - 2)
                freed(act, G_IN[l] + N_IN - 1)
                pt = 0
                outputs = outputs_of(quads)
                for step, (scored, turned) in enumerate(attention_steps(quads)):
                    if step == KEYS_STEP + 4 * len(quads):
                        between_keys(0)
                    if step == QUERIES_STEP + 4 * len(quads):
                        between_queries(0)
                    for _ in turned:
                        act.wait_ge(s["pt_done"], pt + 1)
                        if pt >= 2:
                            act.wait_ge(s["pv_done"], pt - 1)
                        act.activation(prob_t[:, pt % 2, :], bank(4 + pt % 2), ACT.Copy).then_inc(s["pt_copied"], 1)
                        pt += 1
                    if scored:
                        qn, c = scored
                        n, j, keys, nl = quads[qn]
                        st = stat[:, qn % 2]
                        if qn >= 2 and c == 0:
                            act.wait_ge(s["pt_done"], sum(key_blocks[:qn - 1]))
                        it = 4 * qn + c
                        act.wait_ge(s["negmax"], it + 1)
                        w_ = P * len(keys)
                        b0 = 2 * (it % 2) * 512 + 512 - P * nl
                        act.activation(prob[:, qn % 2, c, 0:w_], ps[:, b0:b0 + w_], ACT.Exp,
                                       bias=st[:, 0, c:c + 1], accum_out=st[:, 2, c:c + 1]).then_inc(s["exped"], 1)
                        if c == 3:
                            act.wait_ge(s["esink_in"], qn + 1)
                            act.activation(st[:, 3, :], st[:, 1, :], ACT.Exp).then_inc(s["esink"], 1)
                    if step in outputs:
                        _, n, products = outputs[step]
                        act.wait_ge(s["pv_done"], products)
                        act.activation(act_hi[:, 2:6, n * P:n * P + P], bank(6 + n % 2).rearrange("p (c t) -> p c t", c=4),
                                       ACT.Copy).then_inc(s["o_hi"], 1)

                def copy_keys(c, d):
                    act.wait_ge(s["kt_tr"], 2 * c + d + 1)
                    act.activation(kt[:, d].rearrange("p b k -> p (b k)"), bank(inter_bank(c, d), TOK), ACT.Copy).then_inc(s["kt_copied"], 1)

                def assemble(c):
                    act.wait_ge(s["diag_copied"], LEVELS * (c + 1))
                    for r in range(2):
                        rows = slice(HD * r, HD * r + HD)
                        act.activation(amat[c][rows, 0:nsp, :, rows].rearrange("p b h t -> p (b h) t"), diag[rows, c, 0:nsp].rearrange("p b h t -> p (b h) t"),
                                       ACT.Copy).then_inc(s["amat_ready"], 1)

                def squares_out(c):
                    act.wait_ge(s["o_done"], c + 1)
                    if c > 0:
                        act.wait_ge(s["oy"], c)
                    for n, (t0, t) in enumerate(pp):
                        act.activation(rst[:, t0:t0 + t], bank(6 + n, t), ACT.Square).then_inc(s["osq"], 1)

                def rms_out(c):
                    act.wait_ge(s["oss"], c + 1)
                    for n, (t0, t) in enumerate(pp):
                        act.activation(rst[:, t0:t0 + t], bank(4 + n, t), ACT.Ln, bias=eps_t[:, 0:1], scale=1.0 / HD).then_inc(s["orst_log"], 1)
                    act.wait_ge(s["orst_log"], (c + 1) * len(pp))
                    act.activation(rst[:, 0:T], rst[:, 0:T], ACT.Exp, scale=-0.5).then_inc(s["orst"], 1)

                def split_out(c):
                    act.wait_ge(s["oy"], c + 1)
                    act.activation(act_hi[:, 6 + c, 0:T], gate[:, c, 0:T], ACT.Copy).then_inc(s["oy_hi"], 1)

                exps = 0
                for m in range(2 * (LEVELS + 1) + 1):
                    if m < 2 * (LEVELS + 1) and m % (LEVELS + 1) < LEVELS:
                        exps += 1
                        act.wait_ge(s["d_ready"], 4 * exps)
                        for buf in levels[m % 2][0:2]:
                            act.activation(buf[:, 0:T], buf[:, 0:T], ACT.Exp).then_inc(s["e_ready"], 1)
                    if m > 0:
                        c, v = divmod(m - 1, LEVELS + 1)
                        if v < 2:
                            act.wait_ge(s["a_done"], m)
                            src = bank(2 * ((m - 1) % 2), nsp * P).rearrange("p (n t) -> p n t", t=HD)
                        if v == 0:
                            for r in range(2):
                                rows, other = slice(HD * r, HD * r + HD), slice(HD * (1 - r), HD * (1 - r) + HD)
                                ins = act.activation(amat[c][rows, 0:nsp, :, other].rearrange("p b h t -> p (b h) t"), src[rows], ACT.Copy)
                                ins.then_inc(s["off_copied" if r else "off_half"], 1)
                        if v == 1:
                            act.activation(diag[:, c, 0:nsp].rearrange("p b h t -> p (b h) t"), src, ACT.Copy).then_inc(s["diag_copied"], 1)
                    if m == 0:
                        copy_keys(0, 0)
                        copy_keys(0, 1)
                    if m == 4:
                        between_keys(1)
                    if m == 6:
                        between_queries(1)
                    if m == 8:
                        copy_keys(1, 0)
                    if m == 9:
                        assemble(0)
                    if m == 11:
                        copy_keys(1, 1)
                    if m == 12:
                        squares_out(0)
                    if m == 14:
                        rms_out(0)
                    if m == 16:
                        split_out(0)
                assemble(1)
                squares_out(1)
                rms_out(1)
                split_out(1)

                for i in range(N_OUT):
                    split_hi(W_OUT[l] + i + AHEAD)
                    if i > 0:
                        freed(act, G_OUT[l] + i - 1)
                        square(2 * l + 1, i - 1, (i - 1) % 2)
                freed(act, G_OUT[l] + N_OUT - 1)
                square(2 * l + 1, KC - 1, 1)
                inverse_rms(2 * l + 1)
                split_norm(2 * l + 1, W_UP[l] + AHEAD)

                def up(i):
                    for j in range(4):
                        for w in soon(j)[j == 0:] if isinstance(i, int) else (j + AHEAD,):
                            split_hi(W_UP[l] + w, i, 4, 8 if l == 0 else 4)
                        if l == 0 and j == 0 and not (isinstance(i, int) and i == 0):
                            ada_copy(ADA_BLOCKS - 1, i, 8)
                        g = G_UP[l] + j
                        u = 4 * i + j
                        act.wait_ge(unit_used, W_UP[l] + j + 1 + 4 * i)
                        if l > 0 or j >= 2 or not isinstance(i, int):
                            act.wait_ge(hid32_ready, l * N_UP - 1 + j + 4 * i)
                        for n, (t0, t) in enumerate(pp):
                            act.activation(relu[:, g % 2, t0:t0 + t], bank(g % 2 + 2 * n, t), ACT.Relu, scale=UNSCALE).then_inc(tile_free[g % 2], 2 // len(pp))
                        act.wait_ge(hid32_ready, l * N_UP + 1 + j + 4 * i)
                        act.activation(hid[:, 0, bass.ds(u, 1), 0:T], hid32[:, j % 2, 0:T].unsqueeze(1), ACT.Copy).then_inc(hidhi_ready, 1)

                def down(i, last=False):
                    for j in range(8):
                        if not (last and j >= 8 - AHEAD):
                            split_hi(W_DOWN[l] + j + AHEAD, i, 8, 12 if l == 0 else 8)
                        if l == 0 and j == 0:
                            ada_copy(ADA_BLOCKS + N_UP // 4 - 1, i, 12)
                        if j % 4 == 0:
                            if j == 4:
                                freed(act, G_DOWN[l], 2 * i)
                                square(2 * l + 2, 2 * i, 0)
                            elif not isinstance(i, int) or i > 0:
                                freed(act, G_DOWN[l] + 1, 2 * i - 2)
                                square(2 * l + 2, 2 * i - 1, 1)

                up(0)
                with act.Fori(1, N_UP // 4) as i:
                    up(i)
                down(0)
                with act.Fori(1, N_DOWN // 8 - 1) as i:
                    down(i)
                down(N_DOWN // 8 - 1, l == DEPTH - 1)
                if l == 0:
                    ada_copy(2 * ADA_BLOCKS - 1)
                freed(act, G_DOWN[l] + KC - 1)
                square(2 * l + 2, KC - 1, 1)
            inverse_rms(NORMS - 1)

        @block.vector
        def _(dve):
            links = [0]

            def link(ins):
                links[0] += 1
                ins.then_inc(dve_chain, 1)
                dve.wait_ge(dve_chain, links[0])

            def split_lo(w, i=0, per_w=0):
                n = W_AT[w] if isinstance(i, int) and per_w == 0 else place(W_AT, w, i, per_w, RING)[0]
                dve.wait_ge(hi_ready, w + 1 + per_w * i)
                dve.scalar_tensor_tensor(out=w_lo[:, w % RING, :], in0=stage[:, n % RING, :], scalar=W_SCALE,
                                         in1=w_hi[:, w % RING, :], op0=ALU.mult, op1=ALU.subtract).then_inc(stage_taken[n % RING], 1)

            def ada_mod(l, b, i=0):
                dve.wait_ge(ada_cols, ADA_BLOCKS * l + b + 1 + i)
                at = SMALL["b_ada"][0] + 48 * l + 4 * b + 4 * i
                dve.tensor_tensor(mod[l][:, bass.ds(4 * b + 4 * i, 4), :], bank(7, 8).rearrange("p (k v) -> p k v", v=2),
                                  small[:, bass.ds(at, 4)].unsqueeze(2).broadcast_to([P, 4, 2]), ALU.add).then_inc(mod_ready, 1)

            link(dve.memset(silu_c[:, :, :], 0.0))
            link(dve.memset(eps_t[:, :], EPS))
            link(dve.memset(zeros[:, :], 0.0))
            link(dve.memset(lbt[:, 0, 0, :], 0.0))
            link(dve.memset(lbt[:, 0, 1, :], 1.0))
            dve.wait_ge(small_here, 16)
            lo0, lo1 = sm("lower", 0, 4), sm("lower", 4, 4)
            link(dve.tensor_tensor(lwork[:, 2, :], lo0, lo1, ALU.max))
            link(dve.tensor_tensor(lwork[:, 0, :], lo0, lwork[:, 2, :], ALU.subtract))
            dve.tensor_tensor(lwork[:, 1, :], lo1, lwork[:, 2, :], ALU.subtract).then_inc(setup_v, 1)
            dve.wait_ge(setup_a, 2)
            dve.tensor_tensor(silu_c[:, :, 0:2], sm("c").rearrange("p (k v) -> p k v", v=2), sig_c[:, :, :], ALU.mult).then_inc(setup_done, 1)
            link(dve.tensor_tensor(lwork[:, 0, :], lwork[:, 0, :], lwork[:, 1, :], ALU.add))
            link(dve.reciprocal(lwork[:, 2, :], lwork[:, 0, :]))
            link(dve.tensor_tensor(lbt[:, 1, 0, :], lwork[:, 1, :], lwork[:, 2, :], ALU.mult))
            link(dve.tensor_scalar(lbt[:, 1, 1, :], lbt[:, 1, 0, :], -1.0, 1.0, ALU.mult, ALU.add))
            link(dve.tensor_scalar(nw64[:, :], small[:, SMALL["norm1"][0]:SMALL["norm1"][0] + 4 * KC], A_SCALE, None, ALU.mult))
            link(dve.tensor_scalar(hgw[:, :], sm("hg_norm"), A_SCALE * UNSCALE, None, ALU.mult))
            link(dve.tensor_scalar(neg_sink[:, :], sm("sink"), -1.0, None, ALU.mult))
            dve.tensor_scalar(psc[:, :], sm("pool_scale"), A_SCALE, None, ALU.mult).then_inc(setup_done, 1)
            dve.wait_ge(masks_here, 16)
            dve.tensor_copy(masks[:, :, :], masks32[:, 0:4 * P].rearrange("p (v t) -> p v t", v=8)).then_inc(masks_ready, 1)
            dve.tensor_copy(band[:, :], masks32[:, 4 * P:7 * P]).then_inc(masks_ready, 1)
            dve.wait_ge(masks_ready, 2)
            def make_gains(l, half):
                o = 24 * half
                dve.wait_ge(mod_ready, ADA_BLOCKS * (l + half) + (0 if half else 4))
                for v in range(2):
                    link(dve.scalar_tensor_tensor(out=gains[:, 3 * half, :, v], in0=mod[l][:, o + 8:o + 16, v], scalar=1.0,
                                                  in1=nw64[:, 16 * half + 8 * l:16 * half + 8 * l + KC], op0=ALU.add, op1=ALU.mult))
                link(dve.tensor_scalar(gains[:, 3 * half + 1, :, :], mod[l][:, o:o + 8, :], A_SCALE, None, ALU.mult))

            def make_gate(l, half):
                o = 24 * half + 16
                dve.wait_ge(mod_ready, ADA_BLOCKS * (l + 1))
                link(dve.tensor_scalar(gains[:, 3 * half + 2, :, :], mod[l][:, o:o + 8, :], UNSCALE2 if half else UNSCALE, None, ALU.mult))

            def over_rms(idx, k):
                T = norm_tokens(idx)
                dve.tensor_tensor(h32[:, k, 0:T], x[:, k, 0:T], rst[:, 0:T], ALU.mult).then_inc(h_scaled, 1)

            def norm(idx):
                T = norm_tokens(idx)
                half = idx % 2
                dve.wait_ge(rst_ready, idx + 1)
                if idx == NORMS - 1:
                    for k in range(KC):
                        dve.scalar_tensor_tensor(out=h32[:, k, 0:T], in0=x[:, k, 0:T], scalar=sm("final", k, 1), in1=rst[:, 0:T],
                                                 op0=ALU.mult, op1=ALU.mult).then_inc(out_ready, 1)
                    return
                for k in range(KC + 1):
                    if k < KC and idx > 0:
                        over_rms(idx, k)
                    if k > 0:
                        dve.wait_ge(h_scaled, KC * idx + k)
                        for n, (t0, t) in enumerate(parts(T)):
                            ins = dve.tensor_scalar(h32[:, k - 1, t0:t0 + t], h32[:, k - 1, t0:t0 + t], gains[:, 3 * half, k - 1, n:n + 1],
                                                    gains[:, 3 * half + 1, k - 1, n:n + 1], ALU.mult, ALU.add)
                            if t0 + t == T:
                                ins.then_inc(h32_ready, 1)
                            else:
                                links[0] += 1
                                ins.then_inc(dve_chain, 1)

            for b in range(4):
                if b == 2:
                    dve.wait_ge(rst_ready, 1)
                    for k in range(KC):
                        over_rms(0, k)
                ada_mod(0, b)
            make_gains(0, 0)
            for w in range(AHEAD):
                split_lo(w)

            for l in range(DEPTH):
                s = S[l]
                T = tokens(l)
                pp = parts(T)
                if l > 0:
                    make_gains(l, 0)
                norm(2 * l)
                sigs = ropes = 0
                for i, (name, c) in enumerate(IN_ORDER):
                    g = G_IN[l] + i
                    for w in soon(i):
                        split_lo(W_IN[l] + w)
                    pi = parts(in_tokens(l, name))
                    if name in ("ff", "fb"):
                        gi = 2 * (name == "fb") + c
                        freed(dve, g)
                        dve.tensor_scalar(gbuf[:, gi, :], gbuf[:, gi, :], lbt[:, l, 1, gi:gi + 1], lbt[:, l, 0, gi:gi + 1],
                                          ALU.mult, ALU.add).then_inc(s["f_ready"], 1)
                        dve.wait_ge(s["f_ready"], gi + 1)
                        dve.tensor_scalar(kk[:, gi // 2, gi % 2, :], gbuf[:, gi, :], -1.0, 1.0, ALU.mult, ALU.add).then_inc(s["k_ready"], 1)
                    elif name in ("qh", "gh"):
                        for n, (t0, t) in enumerate(pi):
                            sigs += 1
                            dve.wait_ge(s["sig"], sigs)
                            dst, scale = (qs, UNSCALE) if name == "qh" else (gate, hgw[:, l:l + 1])
                            dve.scalar_tensor_tensor(out=dst[:, c, t0:t0 + t], in0=bank(g % 2 + 2 * n, t), scalar=scale, in1=sgt[:, c, t0:t0 + t],
                                                     op0=ALU.mult, op1=ALU.mult).then_inc(tile_free[g % 2], 2 // len(pi))
                    elif name in ("k", "q"):
                        freed(dve, g)
                        if name == "q":
                            jobs = [(slice(0, P), c)]
                        else:
                            jobs = [(slice(0, HD), 0), (slice(HD, P), 1)]
                        for r, jc in jobs:
                            v = (qa if name == "q" else kpad)[r, jc, 0:LAT]
                            cos, sin = (small[r, SMALL[n][0]:SMALL[n][0] + LAT] for n in ("rope_cos", "rope_sin"))
                            link(dve.stream_shuffle(rot[r, 0, :], v, SWAP))
                            link(dve.tensor_tensor(rot[r, 0, :], rot[r, 0, :], sin, ALU.mult))
                            link(dve.tensor_tensor(rot[r, 1, :], v, cos, ALU.mult))
                            dve.tensor_tensor(v, rot[r, 0, :], rot[r, 1, :], ALU.add).then_inc(s["roped"], 1)
                            ropes += 1
                            dve.wait_ge(s["roped"], ropes)
                    if l == 0 and i % 2 == 0 and i > 0:
                        ada_mod(0, 3 + i // 2)
                    gi = i - SUMS_AT
                    if gi == 2:
                        dve.wait_ge(s["zeroed"], 1)
                    if 0 <= gi < 4:
                        dve.wait_ge(s["g_ready"], gi + 1)
                        for b in range(NB):
                            dst = cum_f[:, gi % 2, b, :] if gi < 2 else cum_b[:, gi % 2, b, 1:P + 1]
                            ins = dve.tensor_tensor_scan(dst, ones, gbuf[:, gi, b * P:(b + 1) * P], 0.0, ALU.mult, ALU.add)
                            if b < NB - 1:
                                links[0] += 1
                                ins.then_inc(dve_chain, 1)
                        ins.then_inc(s["cum_ready"], 1)
                make_gate(l, 0)
                dve.wait_ge(dve_chain, links[0])
                dve.wait_ge(s["cum_ready"], 4)
                nsp = T // P

                def between(c):
                    dve.wait_ge(s["e_inter"], (c + 1) * (NB + nsp + 4))
                    for d in range(2):
                        dve.tensor_tensor(kd[:, d, :], kd[:, d, :], kk[:, d, c, :], ALU.mult).then_inc(s["w_inter"], 1)
                    for d in range(2):
                        dve.tensor_tensor(qi[:, d, 0:T], qi[:, d, 0:T], qs[:, c, 0:T], ALU.mult).then_inc(s["w_inter"], 1)

                quads = quads_of(l < DEPTH - 1)
                outputs = outputs_of(quads)
                for step, (scored, turned) in enumerate(attention_steps(quads)):
                    last = step // 4 - 1
                    sums = step % 4 == 0 and 0 <= last < len(quads)
                    if step == 4 * len(quads) + 2:
                        between(0)
                    if sums:
                        st = stat[:, last % 2]
                        dve.wait_ge(s["esink"], last + 1)
                        link(dve.tensor_tensor(st[:, 4, :], st[:, 2, :], st[:, 3, :], ALU.add))
                        dve.reciprocal(st[:, 5, :], st[:, 4, :]).then_inc(s["rinv"], 1)
                    if scored:
                        qn, c = scored
                        n, j, keys, nl = quads[qn]
                        st = stat[:, qn % 2]
                        at = QH * l + 4 * j
                        if qn >= 2 and c == 0:
                            dve.wait_ge(s["normed"], 2 * (qn - 1))
                            dve.wait_ge(s["normed_v"], 2 * (qn - 1))
                        it = 4 * qn + c
                        dve.wait_ge(s["scores"], it + 1)
                        w_ = P * len(keys)
                        b0 = 2 * (it % 2) * 512 + 512 - P * nl
                        link(dve.tensor_reduce(st[:, 4, c:c + 1], ps[:, b0:b0 + w_], AX_X, ALU.max, negate=True))
                        dve.tensor_tensor(st[:, 0, c:c + 1], st[:, 4, c:c + 1], neg_sink[:, at + c:at + c + 1], ALU.min).then_inc(s["negmax"], 1)
                        if c == 3:
                            dve.wait_ge(s["negmax"], 4 * qn + 4)
                            dve.tensor_tensor(st[:, 1, :], st[:, 0, :], sm("sink", at, 4), ALU.add).then_inc(s["esink_in"], 1)
                    if sums:
                        dve.wait_ge(s["rinv"], last + 1)
                        for c in (2, 3):
                            v = prob[:, last % 2, c, 0:P * len(quads[last][2])]
                            dve.tensor_scalar(v, v, stat[:, last % 2, 5, c:c + 1], A_SCALE, ALU.mult, ALU.mult).then_inc(s["normed_v"], 1)
                    if step in outputs:
                        low, n, _ = outputs[step]
                        dve.wait_ge(s["o_hi"], low + 1)
                        dve.tensor_tensor(act_lo[:, 2:6, n * P:n * P + P], bank(6 + n % 2).rearrange("p (c t) -> p c t", c=4),
                                          act_hi[:, 2:6, n * P:n * P + P], ALU.subtract).then_inc(s["o_lo"], 1)

                dve.wait_ge(s["pv_done"], sum(len(q[2]) for q in quads))

                def states(c, ds):
                    dve.wait_ge(s["p_done"], 2 * c + ds[-1] + 1)
                    if c > 0 and ds[0] == 0:
                        dve.wait_ge(s["s_done"], c)
                    done = c * 10 + ds[0] * 5
                    for m in range(1, NB):
                        for d in ds:
                            order = (F_ORDER, B_ORDER)[d]
                            prev, cur = order[m - 1], order[m]
                            at = own_bank(c, d) * 512 + P * (m - 1)
                            for h in range(2):
                                r = slice(HD * h, HD * h + HD)
                                src = ps[r, at + HD * h:at + HD * h + HD]
                                if m == 1:
                                    ins = dve.tensor_copy(state[r, d, cur, r], src)
                                else:
                                    ins = dve.scalar_tensor_tensor(out=state[r, d, cur, r], in0=state[r, d, prev, r], scalar=dec[r, d, prev:prev + 1],
                                                                   in1=src, op0=ALU.mult, op1=ALU.add)
                                ins.then_inc(s["st_ready" if h else "st_half"], 1)
                        done += len(ds)
                        dve.wait_ge(s["st_half"], done)
                        dve.wait_ge(s["st_ready"], done)

                def gate_out(c):
                    dve.wait_ge(s["osq"], (c + 1) * len(pp))
                    for n, (t0, t) in enumerate(pp):
                        dve.tensor_tensor(gate[:, c, t0:t0 + t], bank(6 + n, t), gate[:, c, t0:t0 + t], ALU.mult).then_inc(s["og"], 1)

                def scale_out(c):
                    dve.wait_ge(s["og"], (c + 1) * len(pp))
                    dve.wait_ge(s["orst"], c + 1)
                    dve.tensor_tensor(gate[:, c, 0:T], gate[:, c, 0:T], rst[:, 0:T], ALU.mult).then_inc(s["oy"], 1)

                def split_out(c):
                    dve.wait_ge(s["oy_hi"], c + 1)
                    dve.tensor_tensor(act_lo[:, 6 + c, 0:T], gate[:, c, 0:T], act_hi[:, 6 + c, 0:T], ALU.subtract).then_inc(s["oy_lo"], 1)

                exps = 0
                for m in range(2 * (LEVELS + 1) + 1):
                    c, v = divmod(m, LEVELS + 1)
                    if c < 2:
                        ek, eq, km, qm = levels[m % 2]
                        if m < 2:
                            link(dve.memset(qm[HD:P, 0, :], 0.0))
                            dve.memset(qm[0:HD, 1, :], 0.0).then_inc(s["rows_zero"], 1)
                        if m >= 2:
                            dve.wait_ge(s["a_done"], m - 1)
                        if v < LEVELS:
                            h = P >> (v + 1)
                            exps += 1
                            dve.wait_ge(s["e_ready"], 2 * exps)
                            for side in range(2):
                                o, e_, k_ = (b.rearrange("p (b s t) -> p b s t", s=2, t=h)[:, :, side] for b in (km[:, 0:T], ek[:, 0:T], kk[:, side, c, 0:T]))
                                dve.tensor_tensor(o, e_, k_, ALU.mult).then_inc(s["m_ready"], 1)
                            for hh in range(2):
                                r = slice(HD * hh, HD * hh + HD)
                                dve.tensor_tensor(qm[r, hh, 0:T], qs[r, c, 0:T], eq[r, 0:T], ALU.mult).then_inc(s["m_ready"], 1)
                        else:
                            dve.tensor_tensor(km[:, 0:T], kk[:, 0, c, 0:T], kk[:, 1, c, 0:T], ALU.add).then_inc(s["m_ready"], 2)
                            for hh in range(2):
                                r = slice(HD * hh, HD * hh + HD)
                                dve.tensor_copy(qm[r, hh, 0:T], qs[r, c, 0:T]).then_inc(s["m_ready"], 1)
                    if m > 0:
                        c, v = divmod(m - 1, LEVELS + 1)
                        if v >= 2:
                            dve.wait_ge(s["a_done"], m)
                            taken(dve, s, m - 2)
                            src = bank(2 * ((m - 1) % 2), nsp * P).rearrange("p (n t) -> p n t", t=HD)
                            dve.copy_predicated(diag[:, c, 0:nsp].rearrange("p b h t -> p (b h) t"), masks[:, v:v + 1, :].broadcast_to([P, 2 * nsp, HD]),
                                                src).then_inc(s["diag_copied"], 1)
                    if m == 2:
                        states(0, (0, 1))
                    if m == 7:
                        between(1)
                    if m == 9:
                        states(1, (0,))
                    if m == 12:
                        states(1, (1,))
                        gate_out(0)
                    if m == 15:
                        scale_out(0)
                    if m == 16:
                        split_out(0)
                gate_out(1)
                scale_out(1)
                split_out(1)

                for i in range(N_OUT):
                    split_lo(W_OUT[l] + i + AHEAD)
                    g = G_OUT[l] + i
                    dve.wait_ge(unit_used, W_OUT[l] + i + 1)
                    for n, (t0, t) in enumerate(pp):
                        dve.scalar_tensor_tensor(out=x[:, i, t0:t0 + t], in0=bank(g % 2 + 2 * n, t), scalar=gains[:, 2, i, n:n + 1],
                                                 in1=x[:, i, t0:t0 + t], op0=ALU.mult, op1=ALU.add).then_inc(tile_free[g % 2], 2 // len(pp))
                make_gains(l, 1)
                make_gate(l, 1)
                norm(2 * l + 1)

                def up(i):
                    for j in range(4):
                        for w in soon(j) if isinstance(i, int) else (j + AHEAD,):
                            split_lo(W_UP[l] + w, i, 4)
                        g = G_UP[l] + j
                        freed(dve, g, 4 * i)
                        if l > 0 or j >= 2 or not isinstance(i, int):
                            dve.wait_ge(hid_ready, l * N_UP - 1 + j + 4 * i)
                        dve.tensor_tensor(hid32[:, j % 2, 0:T], relu[:, g % 2, 0:T], relu[:, g % 2, 0:T], ALU.mult).then_inc(hid32_ready, 1)
                        if l == 0 and j == 0 and not (isinstance(i, int) and i == 0):
                            ada_mod(1, -1, i)

                def down(i, last=False):
                    for j in range(8):
                        if not (last and j >= 8 - AHEAD):
                            split_lo(W_DOWN[l] + j + AHEAD, i, 8)
                        if j % 4 == 3:
                            g = G_DOWN[l] + j // 4
                            dve.wait_ge(unit_used, W_DOWN[l] + j + 1 + 8 * i)
                            for n, (t0, t) in enumerate(pp):
                                xs = x[:, bass.ds(2 * i + j // 4, 1), t0:t0 + t]
                                dve.scalar_tensor_tensor(out=xs, in0=bank(g % 2 + 2 * n, t).unsqueeze(1),
                                                         scalar=gains[:, 5, bass.ds(2 * i + j // 4, 1), n], in1=xs,
                                                         op0=ALU.mult, op1=ALU.add).then_inc(tile_free[g % 2], 2 // len(pp))
                        if l == 0 and j == 0:
                            ada_mod(1, N_UP // 4 - 1, i)

                up(0)
                with dve.Fori(1, N_UP // 4) as i:
                    up(i)
                down(0)
                with dve.Fori(1, N_DOWN // 8 - 1) as i:
                    down(i)
                down(N_DOWN // 8 - 1, l == DEPTH - 1)
                if l == 0:
                    ada_mod(1, ADA_BLOCKS - 1)
            norm(NORMS - 1)

        @block.gpsimd
        def _(pool):
            links = [0]

            def link(ins):
                links[0] += 1
                ins.then_inc(pool_chain, 1)
                pool.wait_ge(pool_chain, links[0])

            def add_squares(idx):
                T = norm_tokens(idx)
                link(pool.memset(sq_sum[:, 0:T], 0.0))
                for k in range(KC - 1):
                    pool.wait_ge(sq_ready, KC * idx + k + 1)
                    if k > 0:
                        pool.wait_ge(sq_added, (KC - 1) * idx + k)
                    pool.tensor_tensor(sq_sum[:, 0:T], sq_sum[:, 0:T], sq[:, k % 2, 0:T], ALU.add).then_inc(sq_added, 1)

            def norm(idx):
                T = norm_tokens(idx)
                for k in range(KC):
                    pool.wait_ge(hhi_ready, KC * idx + k + 1)
                    pool.tensor_tensor(act_lo[:, k, 0:T], h32[:, k, 0:T], act_hi[:, k, 0:T], ALU.subtract).then_inc(act_ready, 1)

            pool.wait_ge(small_here, 16)
            for l in range(DEPTH):
                s = S[l]
                T = tokens(l)
                pp = parts(T)
                if l == 0:
                    add_squares(0)
                norm(2 * l)
                pool.wait_ge(act_ready, KC * (2 * l + 1))
                for c in range(2):
                    for t in (0, 8 + LAT, PADW - 8):
                        ins = pool.memset(pa[:, c, t:t + 8], 0.0)
                        if (c, t) < (1, PADW - 8):
                            link(ins)
                ins.then_inc(s["pads_zero"], 1)
                pool.wait_ge(s["pads_zero"], 1)
                link(pool.memset(kpad[HD:P, 0, :], 0.0))
                link(pool.memset(kpad[0:HD, 1, :], 0.0))
                link(pool.memset(cum_b[:, 0, :, 0:1], 0.0))
                pool.memset(cum_b[:, 1, :, 0:1], 0.0).then_inc(s["zeroed"], 1)
                for c in range(2):
                    freed(pool, G_IN[l] + c)
                    u, a, b = pa[:, c, :], pool_a, pool_b
                    link(pool.tensor_tensor(a[:, 1:PADW], u[:, 0:PADW - 1], u[:, 1:PADW], ALU.add))
                    if c == 1:
                        link(pool.tensor_tensor(b[:, 2:PADW - 1], a[:, 1:PADW - 2], a[:, 3:PADW], ALU.add))
                        link(pool.tensor_tensor(a[:, 4:PADW - 3], b[:, 2:PADW - 5], b[:, 6:PADW - 1], ALU.add))
                        far = 4
                    else:
                        far = 1
                    hi_rows = slice(HD, P)
                    link(pool.tensor_tensor(b[hi_rows, 8:PADW - 8], a[hi_rows, 8 - far:PADW - 8 - far], a[hi_rows, 8 + far:PADW - 8 + far], ALU.add))
                    for r, buf in ((slice(0, HD), a), (hi_rows, b)):
                        for ei, t in enumerate(EDGES):
                            at = SMALL["edge"][0] + 32 * c + 8 * ei
                            link(pool.tensor_tensor(buf[r, t:t + 8], buf[r, t:t + 8], small[r, at:at + 8], ALU.mult))
                        iw = SMALL["inv_window"][0] + c
                        link(pool.tensor_scalar(buf[r, 8:PADW - 8], buf[r, 8:PADW - 8], small[r, iw:iw + 1], 1.0, ALU.mult, ALU.mult))
                        ins = pool.tensor_tensor(pa[r, c, 8:PADW - 8], buf[r, 8:PADW - 8], pa[r, c, 8:PADW - 8], ALU.subtract)
                        if r.start == 0:
                            link(ins)
                        else:
                            ins.then_inc(s["pool_diff"], 1)
                            pool.wait_ge(s["pool_diff"], c + 1)
                for c in range(2):
                    pool.wait_ge(s["pool_hi"], c + 1)
                    pool.tensor_tensor(act_lo[:, c, 0:T], pa[:, c, 0:T], act_hi[:, c, 0:T], ALU.subtract).then_inc(s["pool_lo"], 1)
                pool.wait_ge(s["pool_lo"], 2)
                pool.memset(state[:, :, :, :], 0.0).then_inc(s["state_zero"], 1)
                quads = quads_of(l < DEPTH - 1)
                for qn, (n, j, keys, nl) in enumerate(quads):
                    pool.wait_ge(s["rinv"], qn + 1)
                    for c in (0, 1):
                        v = prob[:, qn % 2, c, 0:P * len(keys)]
                        pool.tensor_scalar(v, v, stat[:, qn % 2, 5, c:c + 1], A_SCALE, ALU.mult, ALU.mult).then_inc(s["normed"], 1)
                nsp = T // P
                pool.wait_ge(s["pv_done"], sum(len(q[2]) for q in quads))
                for m in range(2 * (LEVELS + 1)):
                    c, v = divmod(m, LEVELS + 1)
                    if v == LEVELS:
                        continue
                    h = P >> (v + 1)
                    if m >= 2:
                        pool.wait_ge(s["m_ready"], 4 * (m - 1))
                    ek, eq = (b[:, 0:T].rearrange("p (b n s t) -> p b n s t", b=nsp, s=2, t=h) for b in levels[m % 2][0:2])
                    f, g_ = (b[:, c, 0:nsp, 0:P].rearrange("p b (n s t) -> p b n s t", s=2, t=h) for b in (cum_f, cum_b))
                    shape = [P, nsp, P // (2 * h), h]
                    f_mid = f[:, :, :, 0, h - 1:h].broadcast_to(shape)
                    g_mid = g_[:, :, :, 1, 0:1].broadcast_to(shape)
                    for o, x_, y_ in ((ek[:, :, :, 0], f_mid, f[:, :, :, 0]), (ek[:, :, :, 1], g_[:, :, :, 1], g_mid),
                                      (eq[:, :, :, 0], g_mid, g_[:, :, :, 0]), (eq[:, :, :, 1], f[:, :, :, 1], f_mid)):
                        pool.tensor_tensor(o, x_, y_, ALU.subtract).then_inc(s["d_ready"], 1)
                pool.wait_ge(s["o_done"], 2)
                add_squares(2 * l + 1)
                norm(2 * l + 1)

                def up(i):
                    for j in range(4):
                        u = 4 * i + j
                        pool.wait_ge(hidhi_ready, l * N_UP + 1 + j + 4 * i)
                        pool.tensor_tensor(hid[:, 1, bass.ds(u, 1), 0:T], hid32[:, j % 2, 0:T].unsqueeze(1), hid[:, 0, bass.ds(u, 1), 0:T],
                                           ALU.subtract).then_inc(hid_ready, 1)

                with pool.Fori(0, N_UP // 4) as i:
                    up(i)
                pool.wait_ge(hid_ready, (l + 1) * N_UP)
                add_squares(2 * l + 2)

        @block.tensor
        def _(pe):
            def product(w, g, T, moving, k0, start, stop, i=0, per_w=0, per_n=0, per_g=0):
                n, more = place(W_AT, w, i, per_w, per_n)
                pe.wait_ge(stage_taken[n % RING], n // RING + 1 + more * i)
                if start and g >= 2:
                    pe.wait_ge(tile_free[g % 2], 2 * (g // 2) + per_g * i)
                hi, lo = moving
                for k in range(KC):
                    wh, wl = (b[:, w % RING, k * P:(k + 1) * P] for b in (w_hi, w_lo))
                    for which, (wt, m) in enumerate(((wh, hi), (wh, lo), (wl, hi))):
                        for b, (t0, t) in enumerate(parts(T)):
                            mm = pe.matmul(bank(g % 2 + 2 * b, t), wt, m[:, k0 + k, t0:t0 + t], start=(start and k == 0 and which == 0),
                                           stop=(stop and k == KC - 1 and which == 2), skip_group_check=True)
                mm.then_inc(unit_used, 1)

            def normed(norms):
                return lambda k, lo: pe.wait_ge(act_ready if lo else hhi_ready, KC * norms + k + 1)

            def first_products(w, g, T, before):
                for u in range(2):
                    n = W_AT[w + u]
                    pe.wait_ge(stage_taken[n % RING], n // RING + 1)
                    if g >= 2:
                        pe.wait_ge(tile_free[(g + u) % 2], 2 * ((g + u) // 2))
                for k in range(KC):
                    for lo in range(2):
                        before(k, lo)
                        for u in range(2):
                            wh, wl = (b[:, (w + u) % RING, k * P:(k + 1) * P] for b in (w_hi, w_lo))
                            for wt, m in ((wh, act_lo),) if lo else ((wh, act_hi), (wl, act_hi)):
                                for b, (t0, t) in enumerate(parts(T)):
                                    mm = pe.matmul(bank((g + u) % 2 + 2 * b, t), wt, m[:, k, t0:t0 + t], start=(k == 0 and wt is wh and m is act_hi),
                                                   stop=(k == KC - 1 and lo == 1), skip_group_check=True)
                            if k == KC - 1 and lo:
                                mm.then_inc(unit_used, 1)

            def product_tokens(w, g):
                n = W_AT[w]
                pe.wait_ge(stage_taken[n % RING], n // RING + 1)
                pe.wait_ge(tile_free[g % 2], 2 * (g // 2))
                for b in range(NB):
                    dst = bank(g % 2 + 2 * (b >= LB), P, P * (b % LB))
                    for k in range(KC):
                        wh, wl = (q[:, w % RING, k * P:(k + 1) * P] for q in (w_hi, w_lo))
                        ah, al = (q[:, k, b * P:(b + 1) * P] for q in (act_hi, act_lo))
                        for which, (st, mv) in enumerate(((ah, wh), (ah, wl), (al, wh))):
                            mm = pe.matmul(dst, st, mv, start=(k == 0 and which == 0), stop=(k == KC - 1 and which == 2), skip_group_check=True)
                mm.then_inc(unit_used, 1)

            def ada_unit(a, i=0, per_n=0, per_a=0):
                n, more = place(A_AT, a, i, per_a, per_n)
                pe.wait_ge(stage_full[n % RING], 16 * (n // RING + 1) + 16 * more * i)
                if a % 4 == 0 and a // 4 > 0:
                    pe.wait_ge(ada_copied, a // 4 + (per_a // 4) * i)
                q, kh = a % 4 // 2, a % 2
                for e in range(4):
                    mm = pe.matmul(bank(6, 256, 256 * q)[32 * e:32 * e + 32, :], silu_c[:, 4 * kh + e, :], stage[:, n % RING, 256 * e:256 * e + 256],
                                   start=(kh == 0), stop=(kh == 1), skip_group_check=True)
                mm.then_inc(stage_taken[n % RING], 1)

            def ada_tile(b):
                for a in range(4 * b, 4 * b + 4):
                    ada_unit(a)

            def ada_transpose(b, i=0):
                pe.wait_ge(ada_copied, b + 1 + i)
                if b > 0:
                    pe.wait_ge(mod_ready, b + i)
                for q in range(4):
                    mm = pe.matmul(bank(7, 2, 2 * q), ada_row[:, q * P:(q + 1) * P], sm("sel"), start=True, stop=True, skip_group_check=True)
                mm.then_inc(ada_cols, 1)

            def norm(idx):
                T = norm_tokens(idx)
                pe.wait_ge(sq_added, (KC - 1) * (idx + 1))
                for b, (t0, t) in enumerate(parts(T)):
                    pe.matmul(bank(4 + b, t), ones, sq_sum[:, t0:t0 + t], start=True, stop=False, skip_group_check=True)
                pe.wait_ge(sq_ready, KC * (idx + 1))
                for b, (t0, t) in enumerate(parts(T)):
                    mm = pe.matmul(bank(4 + b, t), ones, sq[:, (KC - 1) % 2, t0:t0 + t], start=False, stop=True, skip_group_check=True)
                mm.then_inc(sq_used, 1)

            def value_product(s, m, n, j, keys, ki):
                pe.wait_ge(s["pt_copied"], m + 1)
                for e in range(2):
                    mm = pe.matmul(bank(6 + n % 2, 2 * P, 2 * P * j)[HD * e:HD * e + HD, :], va[:, keys[ki], HD * j:HD * j + HD],
                                   prob_t[:, m % 2, 2 * P * e:2 * P * e + 2 * P], start=(ki == 0), stop=(ki == len(keys) - 1), skip_group_check=True)
                mm.then_inc(s["pv_done"], 1)

            act = (act_hi, act_lo)
            hidden = (hid[:, 0], hid[:, 1])
            pe.wait_ge(setup_done, 1)
            for b in range(4):
                ada_tile(b)
                ada_transpose(b)
                if b == 1:
                    norm(0)
            for l in range(DEPTH):
                s = S[l]
                T = tokens(l)
                pp = parts(T)
                if l > 0:
                    norm(2 * l)
                for i, (name, c) in enumerate(IN_ORDER):
                    w, g = W_IN[l] + i, G_IN[l] + i
                    if i == 0:
                        first_products(w, g, in_tokens(l, name), normed(2 * l))
                    elif i == 1:
                        pass
                    elif name in TOKEN_MAJOR:
                        product_tokens(w, g)
                    else:
                        product(w, g, in_tokens(l, name), act, 0, True, True)
                    if l == 0 and i % 2 == 0 and i > 0:
                        ada_transpose(3 + i // 2)
                    if l == 0 and i < 16:
                        ada_unit(16 + 2 * i)
                        ada_unit(17 + 2 * i)
                freed(pe, G_IN[l] + N_IN - 2)
                freed(pe, G_IN[l] + N_IN - 1)
                pe.wait_ge(masks_ready, 2)
                for c in range(2):
                    pe.wait_ge(s["pool_diff"], c + 1)
                    for b, (t0, t) in enumerate(pp):
                        mm = pe.matmul(bank(2 * c + b, t), sm("pool_w", (2 * l + c) * P, P), pa[:, c, SEG[b][0]:SEG[b][0] + t], start=True, stop=True,
                                       skip_group_check=True)
                    mm.then_inc(s["pool_mm"], 1)

                quads = quads_of(l < DEPTH - 1)
                pe.wait_ge(s["roped"], 6)
                pe.wait_ge(s["pool_y"], 2 * len(pp))
                if l == 0:
                    pe.wait_ge(mod_ready, ADA_BLOCKS)
                pt = 0
                waiting = []
                for scored, turned in attention_steps(quads):
                    if scored:
                        qn, c = scored
                        n, j, keys, nl = quads[qn]
                        it = 4 * qn + c
                        if it >= 2:
                            pe.wait_ge(s["exped"], it - 1)
                        q = qa[:, c, n * P:n * P + P]
                        b = 2 * (it % 2)
                        if nl:
                            at = 512 - P * nl
                            pe.matmul(bank(b, P * nl, at), q, kpad[:, j, keys[0] * P:keys[0] * P + P * nl], start=True, stop=False, skip_group_check=True)
                            masked = [(kb, m) for kb, m in ((n - 1, 0), (n + 1, 1)) if kb in keys[:nl]]
                            for kb, m in masked:
                                pe.matmul(bank(b, P, at + P * keys.index(kb)), band[:, 0:P], band[:, (1 + m) * P:(2 + m) * P],
                                          start=False, stop=(kb, m) == masked[-1], skip_group_check=True)
                        pe.matmul(bank(b + 1, CTX), q, kpad[:, j, LAT:TOK], start=True, stop=True, skip_group_check=True).then_inc(s["scores"], 1)
                    for m, qn, ki in waiting:
                        n, j, keys, nl = quads[qn]
                        if ki == 0 and j == 0 and qn >= 4:
                            pe.wait_ge(s["o_lo"], qn // 2 - 1)
                        value_product(s, m, n, j, keys, ki)
                    waiting = []
                    for qn, ki in turned:
                        if ki == 0:
                            pe.wait_ge(s["normed"], 2 * (qn + 1))
                            pe.wait_ge(s["normed_v"], 2 * (qn + 1))
                        if pt >= 2:
                            pe.wait_ge(s["pt_copied"], pt - 1)
                        for c in range(4):
                            mm = pe.transpose(bank(4 + pt % 2, P, P * c), prob[:, qn % 2, c, P * ki:P * ki + P], ident)
                        mm.then_inc(s["pt_done"], 1)
                        waiting.append((pt, qn, ki))
                        pt += 1

                nsp = T // P
                pe.wait_ge(s["o_lo"], len(quads) // 2)

                def turn_keys(c, d):
                    pe.wait_ge(s["w_inter"], 4 * c + d + 1)
                    if c > 0 and d == 1:
                        pe.wait_ge(s["st_ready"], 10 * c + 5)
                    for b in range(NB):
                        mm = pe.transpose(bank(inter_bank(c, d), P, b * P), kd[:, d, b * P:b * P + P], ident)
                    mm.then_inc(s["kt_tr"], 1)

                def own_states(c, d):
                    pe.wait_ge(s["kt_copied"], 2 * c + d + 1)
                    for m in range(NB - 1):
                        b = (F_ORDER, B_ORDER)[d][m]
                        mm = pe.matmul(bank(own_bank(c, d), P, m * P), kt[:, d, b, :], hv[:, c, b, :], start=True, stop=True, skip_group_check=True)
                    mm.then_inc(s["p_done"], 1)

                def from_states(c):
                    pe.wait_ge(s["st_ready"], 10 * (c + 1))
                    pe.wait_ge(s["w_inter"], 4 * (c + 1))
                    if c > 0:
                        pe.wait_ge(s["osq"], c * len(pp))
                        pe.wait_ge(s["og"], c * len(pp))
                    for n, (t0, t) in enumerate(pp):
                        pe.matmul(bank(6 + n, t), zeros[:, :], zeros[:, :].unsqueeze(1).broadcast_to([P, t // P, P]), start=True, stop=False, skip_group_check=True)
                    for b in range(nsp):
                        for d, order in enumerate((F_ORDER, B_ORDER)):
                            if b != order[0]:
                                mm = pe.matmul(bank(6 + (b >= LB), P, P * (b % LB)), state[:, d, b, :], qi[:, d, b * P:b * P + P],
                                               start=False, stop=False, skip_group_check=True)
                    mm.then_inc(s["s_done"], 1)

                def from_weights(c):
                    pe.wait_ge(s["amat_ready"], 2 * (c + 1))
                    pe.wait_ge(s["off_copied"], c + 1)
                    for b in range(nsp):
                        dst = bank(6 + (b >= LB), P, P * (b % LB))
                        for h in range(2):
                            r = slice(HD * h, HD * h + HD)
                            mm = pe.matmul(dst[r, :], hv[:, c, b, r], amat[c][:, b, h, :], start=False, stop=True, skip_group_check=True)
                    mm.then_inc(s["o_done"], 1)

                def head_squares(c):
                    pe.wait_ge(s["osq"], (c + 1) * len(pp))
                    pe.wait_ge(s["st_ready"], 20)
                    for b, (t0, t) in enumerate(pp):
                        mm = pe.matmul(bank(4 + b, t), pair_ones, rst[:, t0:t0 + t], start=True, stop=True, skip_group_check=True)
                    mm.then_inc(s["oss"], 1)

                for d in range(2):
                    turn_keys(0, d)
                for d in range(2):
                    own_states(0, d)
                for m in range(2 * (LEVELS + 1)):
                    v = m % (LEVELS + 1)
                    pe.wait_ge(s["m_ready"], 4 * (m + 1))
                    if m >= 2:
                        taken(pe, s, m - 2)
                    if m < 2:
                        pe.wait_ge(s["rows_zero"], m + 1)
                    km, qm = levels[m % 2][2:]
                    for b in range(nsp):
                        for half in range(2):
                            k0, q0 = b * P + HD * half, b * P + HD * (1 - half if v == 0 else half)
                            mm = pe.matmul(bank(2 * (m % 2), P * nsp)[HD * half:HD * half + HD, b * P:b * P + P], km[:, k0:k0 + HD], qm[:, :, q0:q0 + HD],
                                           start=True, stop=True, skip_group_check=True)
                    mm.then_inc(s["a_done"], 1)
                    if m == 3:
                        from_states(0)
                    if m == 7:
                        turn_keys(1, 0)
                    if m == 8:
                        own_states(1, 0)
                    if m == 10:
                        from_weights(0)
                        turn_keys(1, 1)
                    if m == 11:
                        own_states(1, 1)
                    if m == 13:
                        head_squares(0)
                    if m == 14:
                        from_states(1)
                from_weights(1)

                def mixed(k, lo):
                    if lo:
                        return
                    if k == 0:
                        pe.wait_ge(s["pool_lo"], 2)
                        taken(pe, s, 2 * (LEVELS + 1) - 2)
                        taken(pe, s, 2 * (LEVELS + 1) - 1)
                    if k == 3:
                        head_squares(1)
                    if k == 6:
                        pe.wait_ge(s["oy_lo"], 1)
                    if k == 7:
                        pe.wait_ge(s["oy_lo"], 2)

                first_products(W_OUT[l], G_OUT[l], T, mixed)
                for i in range(2, N_OUT):
                    product(W_OUT[l] + i, G_OUT[l] + i, T, act, 0, True, True)
                norm(2 * l + 1)

                def up(i):
                    for j in range(4):
                        if isinstance(i, int) and j < 2:
                            if j == 0:
                                first_products(W_UP[l], G_UP[l], T, normed(2 * l + 1))
                        else:
                            product(W_UP[l] + j, G_UP[l] + j, T, act, 0, True, True, i, 4, 8 if l == 0 else 4, 4)
                        if l == 0:
                            if j == 0 and not (isinstance(i, int) and i == 0):
                                ada_transpose(ADA_BLOCKS - 1, i)
                            ada_unit(4 * ADA_BLOCKS + j, i, 8, 4)

                def down(i):
                    for j in range(8):
                        if isinstance(i, int) and j < 4:
                            pe.wait_ge(hid_ready, l * N_UP + KC * (j + 1))
                        product(W_DOWN[l] + j, G_DOWN[l] + j // 4, T, hidden, KC * (j % 4), j % 4 == 0, j % 4 == 3, i, 8, 12 if l == 0 else 8, 2)
                        if l == 0 and j == 0:
                            ada_transpose(ADA_BLOCKS + N_UP // 4 - 1, i)
                        if l == 0 and j % 2 == 0:
                            ada_unit(4 * ADA_BLOCKS + N_UP + j // 2, i, 12, 4)

                up(0)
                with pe.Fori(1, N_UP // 4) as i:
                    up(i)
                down(0)
                with pe.Fori(1, N_DOWN // 8) as i:
                    down(i)
                if l == 0:
                    ada_transpose(2 * ADA_BLOCKS - 1)
            norm(NORMS - 1)


def _constants():
    p = np.arange(P)
    out = {"sel": np.zeros((P, 2)), "inv_window": np.zeros((P, 2)), "edge": np.zeros((P, 2, 4, 8))}
    out["sel"][np.arange(4) * 32, 0] = 1
    out["sel"][np.arange(4) * 32 + 1, 1] = 1
    for c in range(2):
        for half in range(2):
            w = POOL_WINDOWS[2 * c + half]
            rows = slice(HD * half, HD * half + HD)
            out["inv_window"][rows, c] = 1 / w
            for e, (n, t0) in enumerate(((LAT, 0), (LAT, LAT - 8), (CTX, 0), (CTX, CTX - 8))):
                t = t0 + np.arange(8)
                out["edge"][rows, c, e] = w / (np.minimum(t + w // 2, n) - np.maximum(t - w // 2, 0))
    out["ident"] = np.eye(P)
    out["ones"] = np.ones((P, P))
    out["pair_ones"] = (p[:, None] // HD == p[None, :] // HD)
    t = np.arange(LAT)
    inv = (10000.0 ** (-np.arange(0, HD // 2, 2, dtype=np.float32) / (HD // 2))).astype(np.float32)
    r = p % HD
    place = np.where(r[:, None] < HD // 2, (t // GRID_W)[None, :], (t % GRID_W)[None, :]).astype(np.float32)
    angle = (place * inv[r % 16][:, None]).astype(np.float32)
    out["rope_cos"] = np.cos(angle)
    out["rope_sin"] = np.sin(angle) * np.where(r % 32 < 16, -1, 1)[:, None]
    levels = np.zeros((P, 8, HD))
    s_, t_ = p[:, None] % HD, np.arange(HD)[None, :]
    for v in range(LEVELS):
        h = P >> (v + 1)
        levels[:, v] = (s_ // (2 * h) == t_ // (2 * h)) & (s_ // h != t_ // h)
    levels[:, LEVELS] = s_ == t_
    band = np.zeros((P, 3, P), np.float32)
    band[:, 0] = np.eye(P)
    band[:, 1] = np.where(p[None, :] < p[:, None], -1e30, 0)
    band[:, 2] = np.where(p[None, :] > p[:, None], -1e30, 0)
    return out, np.concatenate([levels.reshape(P, -1), band.reshape(P, -1)], 1).astype(np.float32)


def _rows(w):
    return w.reshape(-1, P, w.shape[1]).transpose(1, 0, 2)


def _layout(i):
    i = {k: np.ascontiguousarray(v) for k, v in i.items()}
    starts = {"pool": 0, "q": 256, "k": 768, "va": 896, "qh": 1024, "ff": 1280, "fb": 1536, "ih": 1792, "gh": 2048}
    pair = lambda at, c: np.concatenate([at + HD * c + np.arange(HD), at + HD * (4 + c) + np.arange(HD)])
    heads = [(4 * j + a, 4 * j + a + 2) for j in range(KVH) for a in range(2)]
    out_rows = np.concatenate([np.arange(256)] + [256 + HD * h + np.arange(HD) for hs in heads for h in hs] + [np.arange(768, D)])
    weights, ada = [], []
    for l in range(DEPTH):
        w_in, w_out = _rows(i["w_in"][l]), _rows(i["w_out"][l][out_rows])
        up, down, wa = _rows(i["w_mlp1"][l]), _rows(i["w_mlp2"][l]), _rows(i["w_ada"][l])
        for name, c in IN_ORDER:
            cols = pair(starts[name], c) if name == "q" else starts[name] + P * c + np.arange(P)
            weights.append(w_in[:, :, cols])
        weights += [w_out[:, :, k * P:k * P + P] for k in range(KC)]
        weights += [up[:, :, k * P:k * P + P] for k in range(FU)]
        weights += [down[:, KC * q:KC * q + KC, k * P:k * P + P] for k in range(KC) for q in range(4)]
        ada += [wa[:, 4 * kh:4 * kh + 4, b * 512 + 256 * q:b * 512 + 256 * q + 256]
                for b in range(ADA_BLOCKS) for q in range(2) for kh in range(2)]
    stream = np.empty((len(STREAM), P, UNIT), np.float32)
    for n, (kind, u) in enumerate(STREAM):
        stream[n] = (weights if kind == "w" else ada)[u].reshape(P, UNIT)
    small = np.zeros((P, N_SMALL), np.float32)

    def put(name, a):
        at, n = SMALL[name]
        small[:, at:at + n] = np.asarray(a, np.float32).reshape(P, n)

    cols = lambda v: np.moveaxis(v.reshape(v.shape[:-1] + (-1, P)), -1, 0)
    put("c", np.stack([cols(i["c"][0]), cols(i["c_ctx"])], -1))
    put("b_ada", cols(i["b_ada"]))
    for name, key in (("norm1", "norm1_w"), ("norm2", "norm2_w"), ("final", "final_norm_w"), ("pool_scale", "pool_scale"), ("lower", "hg_lower")):
        put(name, cols(i[key]))
    put("hg_norm", np.tile(i["hg_norm_w"].T, (2, 1)))
    put("sink", np.tile(i["attn_sink"].reshape(1, -1), (P, 1)))
    blocks = np.zeros((P, DEPTH, 2, P), np.float32)
    for l in range(DEPTH):
        for g in range(4):
            r = slice(HD * (g % 2), HD * (g % 2) + HD)
            blocks[r, l, g // 2, r] = i["pool_w"][l, g]
    put("pool_w", blocks)
    constants, masks = _constants()
    for name, a in constants.items():
        put(name, a)
    xin = np.ascontiguousarray(np.concatenate([i["x"][0], i["ctx"][0]], 0).T)
    return {"stream": stream, "xin": xin, "small": small, "masks": masks}


def kernel(**inputs):
    import concourse.bacc as bacc
    from concourse.bass_utils import run_bass_kernel_spmd

    arrays = _layout({k: np.asarray(v) for k, v in inputs.items()})
    nc = bacc.Bacc("TRN2", target_bir_lowering=False, num_devices=1)
    args = [nc.dram_tensor(f"in_{k}", a.shape, mybir.dt.from_np(a.dtype), kind="ExternalInput").ap() for k, a in arrays.items()]
    out = nc.dram_tensor("result", (D, LAT), F32, kind="ExternalOutput").ap()
    build_program(nc, *args, out)
    r = run_bass_kernel_spmd(nc, [{f"in_{k}": a for k, a in arrays.items()}], core_ids=[0])
    return np.asarray(r.results[0]["result"]).T[None]
```
